# Optimizing a Trainium2 kernel written in Bass

```python
import math
import jax, jax.numpy as jnp
from jax import lax
import numpy as np

D_MODEL = 1024
BATCH = 1
SEQ = 512
DEPTH = 2

N_A = DEPTH // 2
N_B = DEPTH - N_A
CONV_WIDTH = 31
FFN_CONV_WIDTH = 3
D_FF = 2816
N_HEADS = 8
HEAD_DIM = D_MODEL // N_HEADS
WINDOWS = (128, 512, 2048)
DILATIONS = (1, 4, 16)
N_GROUPS = len(WINDOWS)
Q_WIDTH = N_GROUPS * N_HEADS * HEAD_DIM
BLOCK = 128
EPS = 1e-6
NEG_INF = -1e30


def rms_norm(x, g):
    xf = x.astype(jnp.float32)
    y = xf * lax.rsqrt(jnp.mean(xf * xf, axis=-1, keepdims=True) + EPS)
    return (y * g.astype(jnp.float32)).astype(x.dtype)

def layer_norm(x, g, b):
    xf = x.astype(jnp.float32)
    mu = jnp.mean(xf, axis=-1, keepdims=True)
    var = jnp.mean(jnp.square(xf - mu), axis=-1, keepdims=True)
    y = (xf - mu) * lax.rsqrt(var + EPS)
    return (y * g.astype(jnp.float32) + b.astype(jnp.float32)).astype(x.dtype)

def causal_dwconv(x, w, b):
    k, c = w.shape
    y = lax.conv_general_dilated(
        x, w[:, None, :].astype(x.dtype), window_strides=(1,), padding=[(k - 1, 0)],
        dimension_numbers=("NWC", "WIO", "NWC"), feature_group_count=c)
    return y + b

def conformer_conv_module(h, w_in, b_in, dw, dw_b, ln_g, ln_b, w_out, b_out):
    u = h @ w_in + b_in
    u = u[..., :D_MODEL] * jax.nn.sigmoid(u[..., D_MODEL:])
    u = causal_dwconv(u, dw, dw_b)
    u = layer_norm(u, ln_g, ln_b)
    u = jax.nn.silu(u)
    return u @ w_out + b_out

def conv_ffn(h, w_in, dw, dw_b, w_out):
    u = causal_dwconv(h @ w_in, dw, dw_b)
    a, g = u[..., :D_FF], u[..., D_FF:]
    return (jax.nn.silu(g) * a) @ w_out

def dilated_branch(q, k, v, window, dil):
    b, s, h, dh = q.shape
    steps = window // dil
    assert steps <= BLOCK and s % dil == 0
    L = s // dil
    nblk = -(-L // BLOCK)
    lp = nblk * BLOCK

    def to_sub(t):
        t = t.reshape(b, L, dil, h, dh).transpose(0, 2, 3, 1, 4)
        return jnp.pad(t, ((0, 0), (0, 0), (0, 0), (0, lp - L), (0, 0)))

    qs, ks, vs = to_sub(q), to_sub(k), to_sub(v)
    q_blk = qs.reshape(b, dil, h, nblk, BLOCK, dh)

    def band(t):
        tp = jnp.pad(t, ((0, 0), (0, 0), (0, 0), (BLOCK, 0), (0, 0)))
        prev = tp[:, :, :, :lp].reshape(b, dil, h, nblk, BLOCK, dh)
        cur = tp[:, :, :, BLOCK:].reshape(b, dil, h, nblk, BLOCK, dh)
        return jnp.concatenate([prev, cur], axis=-2)

    k_band, v_band = band(ks), band(vs)
    scores = jnp.einsum("brhnqc,brhnkc->brhnqk", q_blk, k_band).astype(jnp.float32)
    scores = scores * (1.0 / math.sqrt(dh))

    blk_i = jnp.arange(nblk)[:, None, None]
    qi = jnp.arange(BLOCK)[None, :, None]
    kk = jnp.arange(2 * BLOCK)[None, None, :]
    dist = qi + BLOCK - kk
    key_pos = blk_i * BLOCK + kk - BLOCK
    valid = (dist >= 0) & (dist <= steps) & (key_pos >= 0)
    scores = jnp.where(valid, scores, NEG_INF)

    m = jnp.max(scores, axis=-1, keepdims=True)
    p = jnp.exp(scores - m)
    den = jnp.sum(p, axis=-1, keepdims=True)
    out = jnp.einsum("brhnqk,brhnkc->brhnqc", p.astype(v.dtype), v_band)
    out = out / den.astype(out.dtype)
    lse = (m + jnp.log(den))[..., 0]

    out = out.reshape(b, dil, h, lp, dh)[:, :, :, :L]
    out = out.transpose(0, 3, 1, 2, 4).reshape(b, s, h, dh)
    lse = lse.reshape(b, dil, h, lp)[:, :, :, :L]
    lse = lse.transpose(0, 3, 1, 2).reshape(b, s, h)
    return out, lse

def dilated_mixture_attention(h, w_q, w_o, k, v):
    b, s, _ = h.shape
    q = (h @ w_q).reshape(b, s, N_GROUPS, N_HEADS, HEAD_DIM)
    outs, lses = [], []
    for g in range(N_GROUPS):
        o, l = dilated_branch(q[:, :, g], k[:, :, g], v[:, :, g], WINDOWS[g], DILATIONS[g])
        outs.append(o)
        lses.append(l)
    outs = jnp.stack(outs, axis=0)
    wts = jax.nn.softmax(jnp.stack(lses, axis=0), axis=0)
    merged = jnp.sum(wts[..., None].astype(outs.dtype) * outs, axis=0)
    return merged.reshape(b, s, N_HEADS * HEAD_DIM) @ w_o

def first_inputs(seed: int = 0) -> dict:
    key = jax.random.key(seed)
    ks = iter(jax.random.split(key, 32))

    def nrm(shape, fan_in):
        return jax.random.normal(next(ks), shape, jnp.float32) * (fan_in ** -0.5)

    def gain(shape):
        return 1.0 + 0.02 * jax.random.normal(next(ks), shape, jnp.float32)

    def bias(shape):
        return 0.01 * jax.random.normal(next(ks), shape, jnp.float32)

    d = D_MODEL
    return {
        "x": jax.random.normal(next(ks), (BATCH, SEQ, d), jnp.float32),
        "mix_pre_g": gain((DEPTH, d)),
        "mix_post_g": gain((DEPTH, d)),
        "ffn_pre_g": gain((DEPTH, d)),
        "ffn_post_g": gain((DEPTH, d)),
        "cm_w_in": nrm((N_A, d, 2 * d), d),
        "cm_b_in": bias((N_A, 2 * d)),
        "cm_dw": nrm((N_A, CONV_WIDTH, d), CONV_WIDTH),
        "cm_dw_b": bias((N_A, d)),
        "cm_ln_g": gain((N_A, d)),
        "cm_ln_b": bias((N_A, d)),
        "cm_w_out": nrm((N_A, d, d), d),
        "cm_b_out": bias((N_A, d)),
        "kv_norm_g": gain((d,)),
        "w_kv": nrm((d, 2 * Q_WIDTH), d),
        "w_q": nrm((N_B, d, Q_WIDTH), d),
        "w_o": nrm((N_B, N_HEADS * HEAD_DIM, d), N_HEADS * HEAD_DIM),
        "ffn_w_in": nrm((DEPTH, d, 2 * D_FF), d),
        "ffn_dw": nrm((DEPTH, FFN_CONV_WIDTH, 2 * D_FF), FFN_CONV_WIDTH),
        "ffn_dw_b": bias((DEPTH, 2 * D_FF)),
        "ffn_w_out": nrm((DEPTH, D_FF, d), D_FF),
    }

def first_block(x, mix_pre_g, mix_post_g, ffn_pre_g, ffn_post_g,
              cm_w_in, cm_b_in, cm_dw, cm_dw_b, cm_ln_g, cm_ln_b, cm_w_out, cm_b_out,
              kv_norm_g, w_kv, w_q, w_o,
              ffn_w_in, ffn_dw, ffn_dw_b, ffn_w_out):
    b, s, _ = x.shape
    k_sh = v_sh = None
    for i in range(DEPTH):
        h = rms_norm(x, mix_pre_g[i])
        if i < N_A:
            y = conformer_conv_module(h, cm_w_in[i], cm_b_in[i], cm_dw[i], cm_dw_b[i],
                                      cm_ln_g[i], cm_ln_b[i], cm_w_out[i], cm_b_out[i])
        else:
            j = i - N_A
            y = dilated_mixture_attention(h, w_q[j], w_o[j], k_sh, v_sh)
        x = x + rms_norm(y, mix_post_g[i])
        h = rms_norm(x, ffn_pre_g[i])
        y = conv_ffn(h, ffn_w_in[i], ffn_dw[i], ffn_dw_b[i], ffn_w_out[i])
        x = x + rms_norm(y, ffn_post_g[i])
        if i == N_A - 1:
            kv = (rms_norm(x, kv_norm_g) @ w_kv).reshape(b, s, 2, N_GROUPS, N_HEADS, HEAD_DIM)
            k_sh, v_sh = kv[:, :, 0], kv[:, :, 1]
    return x


MIX_WIDTH = D_MODEL
QK_NOPE_DIM = 64
QK_ROPE_DIM = 32
V_HEAD_DIM = 64
Q_LORA_RANK = 384
KV_LORA_RANK = 256
ATTN_WIDTH = N_HEADS * V_HEAD_DIM
ROPE_THETA = 10000.0
Q_BLOCK = 128
CONV_WIDTH_2 = MIX_WIDTH - ATTN_WIDTH
CONV_GROUPS = 8
CONV_K = 3
PROJ_SPLITS = (Q_LORA_RANK, KV_LORA_RANK, QK_ROPE_DIM, CONV_WIDTH_2, CONV_WIDTH_2, CONV_WIDTH_2)
PROJ_WIDTH = sum(PROJ_SPLITS)
FFN_RESIDUAL = 0.5
N_MOD = 9


def rms_norm_2(x, g):
    xf = x.astype(jnp.float32)
    y = xf * lax.rsqrt(jnp.mean(xf * xf, axis=-1, keepdims=True) + EPS)
    return (y * g.astype(jnp.float32)).astype(x.dtype)

def modulate(h, shift, scale):
    return h * (1 + scale[:, None, :]) + shift[:, None, :]

def swiglu(h, w_gu, w_down):
    g, u = jnp.split(h @ w_gu, 2, axis=-1)
    return (jax.nn.silu(g) * u) @ w_down

def rope_tables(positions):
    inv_freq = 1.0 / (ROPE_THETA ** (jnp.arange(0, QK_ROPE_DIM, 2, dtype=jnp.float32) / QK_ROPE_DIM))
    ang = positions.astype(jnp.float32)[..., None] * inv_freq
    return jnp.cos(ang), jnp.sin(ang)

def apply_rope(x, cos, sin):
    x1, x2 = jnp.split(x.astype(jnp.float32), 2, axis=-1)
    c, s = cos[:, :, None, :], sin[:, :, None, :]
    return jnp.concatenate([x1 * c - x2 * s, x2 * c + x1 * s], axis=-1).astype(x.dtype)

def causal_attention(q, k, v):
    S = q.shape[1]
    scale = (QK_NOPE_DIM + QK_ROPE_DIM) ** -0.5
    outs = []
    for i in range(S // Q_BLOCK):
        kv_len = (i + 1) * Q_BLOCK
        qi = q[:, i * Q_BLOCK:kv_len]
        s = jnp.einsum('bqhd,bkhd->bhqk', qi, k[:, :kv_len]).astype(jnp.float32) * scale
        q_pos = i * Q_BLOCK + jnp.arange(Q_BLOCK)
        mask = jnp.arange(kv_len)[None, :] <= q_pos[:, None]
        p = jax.nn.softmax(jnp.where(mask, s, -jnp.inf), axis=-1)
        outs.append(jnp.einsum('bhqk,bkhd->bqhd', p.astype(v.dtype), v[:, :kv_len]))
    return jnp.concatenate(outs, axis=1)

def causal_short_conv(u, w):
    S = u.shape[1]
    up = jnp.pad(u, ((0, 0), (CONV_K - 1, 0), (0, 0)))
    y = w[0] * up[:, 0:S]
    for j in range(1, CONV_K):
        y = y + w[j] * up[:, j:j + S]
    return y

def hybrid_mixer(h, cos, sin, w_in, q_a_norm, w_uq, kv_a_norm, w_ukv, conv_w,
                 attn_out_norm, conv_out_norm, w_o):
    B, S, _ = h.shape
    proj = h @ w_in
    offs = np.cumsum(PROJ_SPLITS)[:-1].tolist()
    c_q, c_kv, k_pe, gate_b, gate_c, val = jnp.split(proj, offs, axis=-1)
    q = (rms_norm_2(c_q, q_a_norm) @ w_uq).reshape(B, S, N_HEADS, QK_NOPE_DIM + QK_ROPE_DIM)
    q_nope, q_pe = jnp.split(q, [QK_NOPE_DIM], axis=-1)
    q_pe = apply_rope(q_pe, cos, sin)
    kv = (rms_norm_2(c_kv, kv_a_norm) @ w_ukv).reshape(B, S, N_HEADS, QK_NOPE_DIM + V_HEAD_DIM)
    k_nope, v = jnp.split(kv, [QK_NOPE_DIM], axis=-1)
    k_pe = apply_rope(k_pe[:, :, None, :], cos, sin)
    q_full = jnp.concatenate([q_nope, q_pe], axis=-1)
    k_full = jnp.concatenate([k_nope, jnp.broadcast_to(k_pe, (B, S, N_HEADS, QK_ROPE_DIM))], axis=-1)
    attn = causal_attention(q_full, k_full, v).reshape(B, S, ATTN_WIDTH)
    conv = gate_b * causal_short_conv(gate_c * val, conv_w)
    merged = jnp.concatenate([rms_norm_2(attn, attn_out_norm), rms_norm_2(conv, conv_out_norm)], axis=-1)
    return merged @ w_o

def second_inputs(seed: int = 0) -> dict:
    key = jax.random.key(seed)
    ks = iter(jax.random.split(key, 32))
    L, D = DEPTH, D_MODEL

    def nrm(shape, scale):
        return jax.random.normal(next(ks), shape, jnp.float32) * scale

    def gain(shape):
        return 1.0 + nrm(shape, 0.05)

    x = nrm((BATCH, SEQ, D), 1.0)
    c = nrm((BATCH, D), 1.0)
    offset = jax.random.randint(next(ks), (BATCH, 1), 0, 4096, dtype=jnp.int32)
    positions = offset + jnp.arange(SEQ, dtype=jnp.int32)[None, :]
    return {
        "x": x, "c": c, "positions": positions,
        "w_ada": nrm((L, D, N_MOD * D), 0.3 * D ** -0.5),
        "b_ada": nrm((L, N_MOD * D), 0.01),
        "ffn1_norm": gain((L, D)),
        "ffn1_w_gu": nrm((L, D, 2 * D_FF), D ** -0.5),
        "ffn1_w_down": nrm((L, D_FF, D), D_FF ** -0.5),
        "mix_norm": gain((L, D)),
        "w_in": nrm((L, D, PROJ_WIDTH), D ** -0.5),
        "q_a_norm": gain((L, Q_LORA_RANK)),
        "w_uq": nrm((L, Q_LORA_RANK, N_HEADS * (QK_NOPE_DIM + QK_ROPE_DIM)), Q_LORA_RANK ** -0.5),
        "kv_a_norm": gain((L, KV_LORA_RANK)),
        "w_ukv": nrm((L, KV_LORA_RANK, N_HEADS * (QK_NOPE_DIM + V_HEAD_DIM)), KV_LORA_RANK ** -0.5),
        "conv_w": nrm((L, CONV_K, CONV_WIDTH_2), CONV_K ** -0.5),
        "attn_out_norm": gain((L, ATTN_WIDTH)),
        "conv_out_norm": gain((L, CONV_WIDTH_2)),
        "w_o": nrm((L, MIX_WIDTH, D), MIX_WIDTH ** -0.5),
        "ffn2_norm": gain((L, D)),
        "ffn2_w_gu": nrm((L, D, 2 * D_FF), D ** -0.5),
        "ffn2_w_down": nrm((L, D_FF, D), D_FF ** -0.5),
        "final_norm": gain((D,)),
    }

def second_block(x, c, positions, w_ada, b_ada, ffn1_norm, ffn1_w_gu, ffn1_w_down,
              mix_norm, w_in, q_a_norm, w_uq, kv_a_norm, w_ukv, conv_w,
              attn_out_norm, conv_out_norm, w_o, ffn2_norm, ffn2_w_gu, ffn2_w_down,
              final_norm):
    cos, sin = rope_tables(positions)
    c_act = jax.nn.silu(c)
    for l in range(DEPTH):
        mod = jnp.split(c_act @ w_ada[l] + b_ada[l], N_MOD, axis=-1)
        h = modulate(rms_norm_2(x, ffn1_norm[l]), mod[0], mod[1])
        x = x + FFN_RESIDUAL * (1 + mod[2])[:, None, :] * swiglu(h, ffn1_w_gu[l], ffn1_w_down[l])
        h = modulate(rms_norm_2(x, mix_norm[l]), mod[3], mod[4])
        y = hybrid_mixer(h, cos, sin, w_in[l], q_a_norm[l], w_uq[l], kv_a_norm[l], w_ukv[l],
                         conv_w[l], attn_out_norm[l], conv_out_norm[l], w_o[l])
        x = x + (1 + mod[5])[:, None, :] * y
        h = modulate(rms_norm_2(x, ffn2_norm[l]), mod[6], mod[7])
        x = x + FFN_RESIDUAL * (1 + mod[8])[:, None, :] * swiglu(h, ffn2_w_gu[l], ffn2_w_down[l])
    return rms_norm_2(x, final_norm)


def setup_inputs(seed=0):
    out = dict(first_inputs(seed))
    for name, value in second_inputs(seed + 1).items():
        if name != "x":
            out[name + "_2"] = value
    return out


def reference(
    x, mix_pre_g, mix_post_g, ffn_pre_g, ffn_post_g, cm_w_in, cm_b_in, cm_dw, cm_dw_b, cm_ln_g,
    cm_ln_b, cm_w_out, cm_b_out, kv_norm_g, w_kv, w_q, w_o, ffn_w_in, ffn_dw, ffn_dw_b,
    ffn_w_out, c_2, positions_2, w_ada_2, b_ada_2, ffn1_norm_2, ffn1_w_gu_2, ffn1_w_down_2,
    mix_norm_2, w_in_2, q_a_norm_2, w_uq_2, kv_a_norm_2, w_ukv_2, conv_w_2, attn_out_norm_2,
    conv_out_norm_2, w_o_2, ffn2_norm_2, ffn2_w_gu_2, ffn2_w_down_2, final_norm_2,
):
    x = first_block(
        x, mix_pre_g, mix_post_g, ffn_pre_g, ffn_post_g, cm_w_in, cm_b_in, cm_dw, cm_dw_b,
        cm_ln_g, cm_ln_b, cm_w_out, cm_b_out, kv_norm_g, w_kv, w_q, w_o, ffn_w_in, ffn_dw,
        ffn_dw_b, ffn_w_out,
    )
    return second_block(
        x, c_2, positions_2, w_ada_2, b_ada_2, ffn1_norm_2, ffn1_w_gu_2, ffn1_w_down_2,
        mix_norm_2, w_in_2, q_a_norm_2, w_uq_2, kv_a_norm_2, w_ukv_2, conv_w_2, attn_out_norm_2,
        conv_out_norm_2, w_o_2, ffn2_norm_2, ffn2_w_gu_2, ffn2_w_down_2, final_norm_2,
    )


_drawn_inputs = setup_inputs


def setup_inputs(seed=0):
    import zlib

    import numpy as np

    out = dict(_drawn_inputs(seed))
    spreads = {}
    factors = {'ffn_post_g': 3.15,
     'cm_b_in': 3.671,
     'cm_ln_b': 3.387,
     'kv_norm_g': 3.373,
     'ffn_dw_b': 3.84,
     'b_ada_2': 3.293,
     'ffn1_norm_2': 3.901,
     'q_a_norm_2': 8.0,
     'attn_out_norm_2': 2.736,
     'conv_out_norm_2': 2.693,
     'ffn2_norm_2': 4.366}
    for name, (base, spread) in spreads.items():
        noise = np.random.default_rng([zlib.crc32(name.encode()), seed]).standard_normal(out[name].shape)
        drawn = base * np.exp(spread * noise) if base else spread * noise
        out[name] = __import__('jax').numpy.asarray(drawn.astype(out[name].dtype))
    for name, factor in factors.items():
        out[name] = (out[name] * factor).astype(out[name].dtype)
    return out
```

```python
from contextlib import ExitStack, contextmanager

import numpy as np

import concourse.bass as bass
from concourse import mybir

F32 = mybir.dt.float32
F32R = mybir.dt.float32r
I32 = mybir.dt.int32
ALU = mybir.AluOpType
ACT = mybir.ActivationFunctionType
AX_X = mybir.AxisListType.X

P = 128
D, S = 1024, 512
KD = D // P
D_FF = 2816
KF = D_FF // P
HEADS, DH = 8, 128
GROUPS = 3
WINDOWS, DILATIONS = (128, 512, 2048), (1, 4, 16)
TAPS, FTAPS = 31, 3
TAPS_PE = 12
Q_RANK, KV_RANK, NOPE, ROPE, VD = 384, 256, 64, 32, 64
KQ, KKV = Q_RANK // P, KV_RANK // P
EPS = 1e-6
NEG = -1e30
RING = 4
ST = 4
SLABW = ST * P
QB = S // P
NMOD = 9
ADA_CHUNK = 512
ADA_CHUNKS = NMOD * D // ADA_CHUNK

STAGES = [("cm_in", 16, 2), ("cm_out", 8, 2), ("f0_in", 44, 2), ("f0_out", 8, 6),
          ("kvq", 72, 2), ("att_o", 8, 2), ("f1_in", 44, 2), ("f1_out", 8, 6)]
for _l in range(2):
    STAGES += [(f"a{_l}_in", 44, 2), (f"a{_l}_out", 8, 6), (f"m{_l}_in", 18, 2), (f"m{_l}_up", 16, 1),
               (f"m{_l}_o", 8, 2), (f"b{_l}_in", 44, 2), (f"b{_l}_out", 8, 6)]
BASE = {}
_s = _t = 0
for _name, _n, _spt in STAGES:
    BASE[_name] = (_s, _t, _spt)
    _s += _n * _spt
    _t += _n
SLABS = _s

COLS = {}
_c = 0
for _name, _n in ([("x_mixpre", 2 * KD), ("mixpost", 2 * KD), ("ffnpre", 2 * KD), ("ffnpost", 2 * KD),
                   ("cm_b_in", 16), ("cm_dw", KD * TAPS), ("cm_dw_b", KD), ("cm_ln_g", KD), ("cm_ln_b", KD),
                   ("cm_b_out", KD), ("kv_g", KD), ("ffn_dw", 2 * 44 * FTAPS), ("ffn_dw_b", 2 * 44),
                   ("c", KD), ("b_ada", 2 * 72), ("ffn1_g", 2 * KD), ("mix_g", 2 * KD), ("q_a", 2 * KQ),
                   ("kv_a", 2 * KKV), ("conv_w", 2 * 4 * FTAPS), ("an_g", 2 * 4), ("cn_g", 2 * 4),
                   ("ffn2_g", 2 * KD), ("final_g", KD), ("inv_freq", 1), ("rope_sign", 1)]):
    COLS[_name] = (_c, _n)
    _c += _n
NCOLS = _c


def blocks1(i):
    return [(g, kb) for g in range(GROUPS) for kb in range(max(0, i - 1) if g == 0 else 0, i + 1)]


CHUNKS1 = [(i, list(enumerate(blocks1(i)))[c:c + 4]) for i in range(QB) for c in range(0, len(blocks1(i)), 4)]


class Signal:

    def __init__(self, handle, name):
        self.handle, self.name, self.n = handle, name, 0


class Counts:

    def __init__(self, known, signals):
        self.known, self.signals = known, signals
        self.table = {"loops": []}
        self.loop_ = None

    def mark(self, ins, sig, keys=(), it=None, ago=0):
        ins.then_inc(sig.handle, 1)
        sig.n += 1
        for key in (keys,) if isinstance(keys, str) else keys:
            if self.loop_ is None:
                named = self.table.setdefault(key, {})
                assert it not in named, key
                named[it] = (sig.name, sig.n)
            else:
                self.loop_["pending"].append((key, sig, sig.n, ago))

    def note(self, key, sig):
        self.table[key] = {None: (sig.name, sig.n)}

    @contextmanager
    def loop(self, eng, start, end):
        before = {s.name: s.n for s in self.signals.values()}
        number = len(self.table["loops"])
        self.table["loops"].append(None)
        with eng.Fori(start, end) as i:
            self.loop_ = {"pending": [], "i": i, "start": start, "number": number}
            yield i
        per = {s.name: s.n - before[s.name] for s in self.signals.values()}
        self.table["loops"][number] = per
        for key, sig, n, ago in self.loop_["pending"]:
            self.table.setdefault(key, {})["loop"] = (sig.name, n + per[sig.name] * (ago - start), per[sig.name])
        for s in self.signals.values():
            s.n = before[s.name] + per[s.name] * (end - start)
        self.loop_ = None

    def last(self, sig, back=0):
        if self.known is None:
            return sig.handle, 1
        if self.loop_ is None:
            return sig.handle, sig.n - back
        per = self.known["loops"][self.loop_["number"]][sig.name]
        return sig.handle, self.loop_["i"] * per + (sig.n - back - per * self.loop_["start"])

    def at(self, key, it=None):
        if self.known is None:
            return next(iter(self.signals.values())).handle, 1
        e = self.known[key]
        if it is None or (isinstance(it, int) and it in e):
            name, n = e[it]
            return self.signals[name].handle, n
        if "loop" not in e:
            name, n = e[None]
            return self.signals[name].handle, n
        name, n, per = e["loop"]
        return self.signals[name].handle, it * per + n


def T(buf, k, w=S):
    if isinstance(k, int):
        return buf[:, k * w:(k + 1) * w]
    return buf[:, bass.ds(k * w, w)]


def build(nc, a, out, known):
    with ExitStack() as ctx:
        def sb(name, shape, dt=F32):
            return ctx.enter_context(nc.sbuf_tensor(name, shape, dt))

        def sem(name):
            return ctx.enter_context(nc.semaphore(name))

        raw = sb("w_raw_ring", [P, RING * SLABW])
        whi = sb("w_hi_ring", [P, RING * SLABW], F32R)
        wlo = sb("w_lo_ring", [P, RING * SLABW], F32R)
        x = sb("x", [P, KD * S])
        hhi = sb("h_hi", [P, KD * S], F32R)
        hlo = sb("h_lo", [P, KD * S], F32R)
        y = sb("y", [P, KD * S])
        cols = sb("cols", [P, NCOLS])
        ident = sb("ident", [P, P])
        ones = sb("ones", [P, 1])
        tables = sb("tables", [P, 3 * S])
        tmp = [sb(f"tmp{j}", [P, S + FTAPS - 1]) for j in range(4)]
        bc = sb("bc", [P, S])
        acc = sb("acc", [P, S])
        small = sb("small", [P, 44])
        modc = sb("mod", [P, 2 * 72])
        derived = sb("mod_derived", [P, 2 * 6 * KD])
        ada_w = sb("ada_w", [P, 2 * ADA_CHUNK])
        ada_acc = sb("ada_acc", [P, ADA_CHUNK])
        ada_full = sb("ada_full", [P, ADA_CHUNK])
        arena_bytes = 2 * KF * S * 4
        arena_base = nc.sbuf_base
        sb("arena", [P, arena_bytes // 4])
        A0 = arena_base
        used = [0]

        def at_arena(name, shape, dt=F32):
            size = int(np.prod(shape[1:])) * 4
            t = nc.alloc_sbuf_tensor_at(name, shape, dt, offset=A0 + used[0])
            used[0] += size
            assert used[0] <= arena_bytes, (name, used[0])
            return t

        mhi = at_arena("mid_hi", [P, KF * S], F32R)
        mlo = at_arena("mid_lo", [P, KF * S], F32R)
        used[0] = 0
        diag = at_arena("tap_diagonals", [P, 2 * TAPS_PE * P])
        ucv = [at_arena(f"gated{q}", [P, S + 32]) for q in range(2)]
        used[0] = 0
        qhi = at_arena("q_in_hi", [P, KD * S], F32R)
        qlo = at_arena("q_in_lo", [P, KD * S], F32R)
        kT1 = at_arena("kT1", [P, 2 * GROUPS * S])
        qT1 = at_arena("qT1", [P, GROUPS * S])
        vT1 = at_arena("vT1", [P, S])
        V1 = at_arena("v1", [P, 2 * GROUPS, QB, P])
        Pr1 = at_arena("probs1", [P, 2 * 10 * P])
        PT1 = at_arena("probsT1", [P, 2 * S])
        used[0] = 0
        cq = at_arena("cq", [P, KQ * S])
        ckv = at_arena("ckv", [P, KKV * S])
        cqhi = at_arena("cq_hi", [P, KQ * S], F32R)
        cqlo = at_arena("cq_lo", [P, KQ * S], F32R)
        ckhi = at_arena("ckv_hi", [P, KKV * S], F32R)
        cklo = at_arena("ckv_lo", [P, KKV * S], F32R)
        bcq = at_arena("bc_q", [P, S])
        bckv = at_arena("bc_kv", [P, S])
        conv = at_arena("conv", [P, 4 * S])
        am = at_arena("attn_out", [P, 4 * S])
        qT2 = at_arena("qT2", [P, 2 * S])
        kT2 = at_arena("kT2", [P, 2 * S])
        kvT2 = at_arena("kvT2", [P, 2 * S])
        V2 = at_arena("v2", [P, 2, QB, P])
        Pr2 = at_arena("probs2", [P, 2 * 10 * P])
        PT2 = at_arena("probsT2", [P, 2 * S])

        banks = [ctx.enter_context(nc.psum_tensor(f"bank{j}", [P, S], F32)) for j in range(8)]
        BCAST, STAT = banks[6], banks[7]

        raw_in = [sem(f"raw_in{j}") for j in range(RING)]
        w_hi = sem("w_hi")
        w_lo = sem("w_lo")
        slab_used = sem("slab_used")
        const_in = sem("const_in")
        table_in = sem("table_in")
        pos_in = sem("pos_in")
        stored = sem("stored")
        passed = sem("passed")
        ada_in = [sem("ada_in0"), sem("ada_in1")]
        diag_ready = sem("diag_ready")
        taps_done = sem("taps_done")
        pool_passed = sem("pool_passed")
        ada_step = sem("ada_step")
        ada_ready = sem("ada_ready")
        ada_sum = sem("ada_sum")
        ada_mod = sem("ada_mod")
        sigs = {n: Signal(sem(n), n) for n in
                ("vec_done", "act_done", "pe_norm", "pe_scores", "pe_turned", "pe_pv")}
        vec, actd, pen, pes, pet, pev = sigs.values()
        K = Counts(known, sigs)
        mark, at = K.mark, K.at
        block = ctx.enter_context(nc.Block())

        def col(name, j=0, n=1):
            c = COLS[name][0]
            return cols[:, c + j:c + j + n]

        def dcol(name, j):
            c = COLS[name][0]
            return cols[:, bass.ds(j + c, 1)]

        def raw_value(base, per, i, j):
            return i * (per // RING * 16) + (base // RING + j // RING + 1) * 16

        NCONST = 6
        @block.sync
        def _(sp):
            sp.dma_start(cols[:, :], a["cols"]).then_inc(const_in, 16)
            for k in range(4):
                sp.dma_start(T(x, k, 2 * S), T(a["x"], k, 2 * S)).then_inc(const_in, 16)
            sp.dma_start(ident[:, :], a["ident"]).then_inc(const_in, 16)
            for j in range(RING):
                sp.dma_start(T(raw, j, SLABW), a["w"][j]).then_inc(raw_in[j], 16)

            def stream(first, end):
                with sp.Fori(first, end) as i:
                    for j in range(RING):
                        sp.wait_ge(w_lo, i * RING + (j + 1))
                        sp.dma_start(T(raw, j, SLABW), a["w"][i * RING + (RING + j)]).then_inc(raw_in[j], 16)

            sp.dma_start(tables[:, 0:256 + 2 * S], a["masks1"]).then_inc(table_in, 16)
            after_att = BASE["f1_in"][0] // RING
            stream(0, after_att)
            sp.wait_ge(*at("att.last"))
            sp.dma_start(tables[:, 0:S], a["causal"]).then_inc(pos_in, 16)
            sp.dma_start(tables[64:96, S:2 * S].bitcast(I32), a["pos"].to_broadcast([ROPE, S])).then_inc(pos_in, 16)
            stream(after_att, SLABS // RING)
            for k in range(KD):
                sp.wait_ge(*at(f"final.y{k}"))
                sp.dma_start(T(out, k), T(y, k)).then_inc(stored, 16)
            sp.wait_ge(stored, 16 * KD)

        @block.gpsimd
        def _(pool):
            pool.wait_ge(const_in, 16 * NCONST)

            def diagonals(i, q):
                c = COLS["cm_dw"][0]
                w = cols[:, bass.ds(i * (2 * TAPS) + (c + q * TAPS), TAPS_PE)]
                nc.gpsimd.tensor_tensor(
                    diag[:, q * TAPS_PE * P:(q + 1) * TAPS_PE * P].rearrange("p (t f) -> p t f", t=TAPS_PE),
                    ident[:, :].unsqueeze(1).to_broadcast([P, TAPS_PE, P]),
                    w.unsqueeze(2).to_broadcast([P, TAPS_PE, P]), ALU.mult).then_inc(diag_ready, 1)

            for q in range(2):
                diagonals(0, q)
            with pool.Fori(1, 4) as i:
                for q in range(2):
                    pool.wait_ge(taps_done, i * 2 + (q - 1))
                    pool.sem_inc(pool_passed, 1)
                    diagonals(i, q)

            pool.wait_ge(*at("silu_c"))
            steps = 2 * KD - 2

            def load(ch, k):
                pool.dma_start(T(ada_w, k % 2, ADA_CHUNK), a["ada"][ch * KD + k]).then_inc(ada_in[k % 2], 16)

            def chunk(ch, last):
                first = isinstance(ch, int) and ch == 0
                for k in range(KD):
                    if k >= 1:
                        pool.wait_ge(ada_step, ch * steps + (2 * k - 1))
                    elif not first:
                        pool.wait_ge(ada_ready, ch)
                    if k + 1 < KD:
                        load(ch, k + 1)
                    elif not last:
                        load(ch + 1, 0)
                    pool.wait_ge(ada_in[k % 2], ch * (16 * KD // 2) + 16 * (k // 2 + 1))
                    c, w = small[:, k:k + 1].to_broadcast([P, ADA_CHUNK]), T(ada_w, k % 2, ADA_CHUNK)
                    if k == 0:
                        nc.gpsimd.tensor_tensor(ada_acc[:, :], w, c, ALU.mult).then_inc(ada_step, 1)
                        continue
                    nc.gpsimd.tensor_tensor(w, w, c, ALU.mult).then_inc(ada_step, 1)
                    pool.wait_ge(ada_step, ch * steps + 2 * k)
                    if k == KD - 1 and not first:
                        pool.wait_ge(ada_sum, ch)
                    dst, done = (ada_acc, ada_step) if k + 1 < KD else (ada_full, ada_ready)
                    nc.gpsimd.tensor_tensor(dst[:, :], ada_acc[:, :], w, ALU.add).then_inc(done, 1)

            load(0, 0)
            chunk(0, False)
            with pool.Fori(1, 2 * ADA_CHUNKS - 1) as ch:
                chunk(ch, False)
            chunk(2 * ADA_CHUNKS - 1, True)

        @block.tensor
        def _(pe):
            def product(stage, i, per_turn, j, kt, ops, bank, nbanks, ready=None):
                s0, _, spt = BASE[stage]
                sl = spt * j
                s = i * (per_turn * spt) + (s0 + sl)
                if j >= nbanks:
                    pe.wait_ge(*at(f"{stage}.read{j - nbanks}", i))
                elif not isinstance(i, int) or i > 0:
                    pe.wait_ge(*at(f"{stage}.read{j - nbanks + per_turn}", i - 1))
                o = bank[:, :]
                for k in range(kt):
                    slot = (sl + k // ST) % RING
                    if k % ST == 0:
                        pe.wait_ge(w_lo, s + (k // ST + 1))
                    if ready is not None:
                        pe.wait_ge(*at(ready.format(k=k)))
                    wh, wl = T(whi, slot * ST + k % ST, P), T(wlo, slot * ST + k % ST, P)
                    hi, lo = ops(k)
                    nc.tensor.matmul(o, wh, hi, start=(k == 0), stop=False)
                    nc.tensor.matmul(o, wh, lo, start=False, stop=False)
                    mm = nc.tensor.matmul(o, wl, hi, start=False, stop=(k == kt - 1))
                    if k % ST == ST - 1 or k == kt - 1:
                        mm.then_inc(slab_used, 1)

            h_ops = lambda k: (T(hhi, k), T(hlo, k))
            m_ops = lambda k: (T(mhi, k), T(mlo, k))
            q_ops = lambda k: (T(qhi, k), T(qlo, k))

            def norm_sum(key):
                pe.wait_ge(*at(f"{key}.acc"))
                for b in range(QB):
                    mm = nc.tensor.matmul(STAT[:, b:b + 1], acc[:, b * P:(b + 1) * P], ones[:, 0:1],
                                          start=True, stop=True)
                mark(mm, pen, f"{key}.sum")

            def norm_bcast(key):
                pe.wait_ge(*at(f"{key}.rstd"))
                for b in range(QB):
                    mm = nc.tensor.matmul(BCAST[:, b * P:(b + 1) * P], small[:, 12 + b:13 + b].to_broadcast([P, P]),
                                          ident[:, :], start=True, stop=True)
                mark(mm, pen, f"{key}.bcast")

            def norm(key):
                norm_sum(key)
                norm_bcast(key)

            def ada(ch):
                pe.wait_ge(ada_ready, ch + 1)
                pe.wait_ge(ada_mod, ch + 1)
                for b in range(4):
                    mm = nc.tensor.matmul(STAT[:, 8 + b:9 + b], ada_full[:, b * P:(b + 1) * P], ones[:, 0:1],
                                          start=True, stop=True)
                mm.then_inc(ada_sum, 1)

            def wide_in(stage, tiles, nkey=None, ada0=None):
                def body(i):
                    for j in range(4):
                        product(stage, i, 4, j, KD, h_ops, banks[j], 4, f"{stage}.h{{k}}" if isinstance(i, int) and i == 0 else None)
                        if isinstance(i, int) and i == 0 and j == 0 and nkey:
                            norm(nkey)
                body(0)
                if ada0 is None:
                    with K.loop(pe, 1, tiles // 4) as i:
                        body(i)
                else:
                    with K.loop(pe, 1, 10) as i:
                        body(i)
                        ada(i + (ada0 - 1))
                    body(10)

            def narrow(stage, kt, ops, ready=None):
                with K.loop(pe, 0, 2) as i:
                    for j in range(4):
                        product(stage, i, 4, j, kt, ops, banks[j], 4, ready)

            pe.wait_ge(const_in, 16 * NCONST)
            pe.wait_ge(*at("ones"))

            def products(i, q):
                for j in (2 * q, 2 * q + 1):
                    product("cm_in", i, 4, j, KD, h_ops, banks[j], 4, "cm_in.h{k}" if isinstance(i, int) and i == 0 else None)
                    if isinstance(i, int) and i == 0 and j == 0:
                        norm("n.cm")

            def taps(i, q):
                pe.wait_ge(diag_ready, i * 2 + (q + 1))
                pe.wait_ge(*at(f"cm.u.{q}", i))
                if not (isinstance(i, int) and i == 0):
                    pe.wait_ge(*at(f"cm.sum.{q}", i - 1))
                for tap in range(TAPS_PE):
                    mm = nc.tensor.matmul(banks[4 + q][:, :], T(diag, q * TAPS_PE + tap, P), ucv[q][:, tap:tap + S],
                                          start=(tap == 0), stop=(tap == TAPS_PE - 1))
                mm.then_inc(taps_done, 1)

            products(0, 0)
            products(0, 1)
            taps(0, 0)
            with K.loop(pe, 1, 4) as i:
                products(i, 0)
                taps(i - 1, 1)
                products(i, 1)
                taps(i, 0)
            taps(3, 1)
            pe.wait_ge(*at("ln.mean_acc"))
            mark(nc.tensor.matmul(BCAST[:, :], ones[:, 0:1].to_broadcast([P, P]), acc[:, :], start=True, stop=True), pen, "ln.mean")
            norm("n.ln")
            narrow("cm_out", KD, h_ops, "cm_out.h{k}")
            norm("n.cmpost")
            wide_in("f0_in", 44, "n.f0", 0)
            narrow("f0_out", KF, m_ops, "f0_in.mid_end")
            norm("n.f0post")

            def scores1(i, it, par):
                for g in range(GROUPS):
                    u = GROUPS * i + g
                    k0 = max(0, i - 1) if g == 0 else 0
                    if i == 0 and g == 0:
                        pe.wait_ge(*at(f"qT{GROUPS - 1}.{par}", it if par == 0 else it - 1))
                        pe.wait_ge(*at(f"V{GROUPS - 1}.{par}", it if par == 0 else it - 1))
                    if u >= 3:
                        pe.wait_ge(*at(f"masked{u - 3}.{par}", it))
                    mm = nc.tensor.matmul(banks[2 + u % 3][:, 0:(i + 1 - k0) * P], T(qT1, g * QB + i, P),
                                          kT1[:, ((par * GROUPS + g) * QB + k0) * P:((par * GROUPS + g) * QB + i + 1) * P], start=True, stop=True)
                    mark(mm, pes, f"scores{u}.{par}", it)

            def turn(c, it, par, chunks, Pr):
                i, bl = chunks[c]
                pe.wait_ge(*at(f"probs{i}.{par}", it))
                if c >= 2:
                    pe.wait_ge(*at(f"PT{c - 2}.{par}", it))
                for n, (m, _) in enumerate(bl):
                    mm = nc.tensor.transpose(banks[5 + c % 2][:, n * P:(n + 1) * P], Pr(i, m), ident[:, :])
                mark(mm, pet, f"turned{c}.{par}", it)

            def pv1(c, it, par):
                i, bl = CHUNKS1[c]
                pe.wait_ge(*at(f"PT{c}.{par}", it))
                if c == 0 and not (isinstance(it, int) and it == 0):
                    pe.wait_ge(*at(f"merged.{1 - par}", it if par == 0 else it - 1))
                for n, (_, (g, kb)) in enumerate(bl):
                    mm = nc.tensor.matmul(banks[7][:, i * P:(i + 1) * P], V1[:, par * GROUPS + g, kb, :],
                                          T(PT1, c % 2 * QB + n, P), start=(c == 0 and n == 0),
                                          stop=(c == len(CHUNKS1) - 1 and n == len(bl) - 1), skip_group_check=True)
                mark(mm, pev, f"pv{c}.{par}", it)

            def head1(it, par, tiles, attn):
                pp = 1 - par
                prob = lambda i, m: T(Pr1, i % 2 * 10 + m, P)
                tr = lambda c: turn(c, it, pp, CHUNKS1, prob)
                plan = {2: [("t", 0)], 3: [("v", 0), ("t", 1), ("t", 2), ("v", 1)],
                        4: [("v", 2), ("VT", 0), ("t", 3), ("t", 4), ("v", 3)],
                        5: [("v", 4), ("VT", 1), ("t", 5), ("t", 6), ("v", 5), ("t", 7), ("v", 6)],
                        6: [("v", 7), ("VT", 2)]}
                for slot in range(9):
                    if tiles:
                        j = 9 * par + slot
                        product("kvq", it, 18, j, KD, q_ops if slot >= 6 else h_ops, banks[j % 2], 2,
                                ("kvq.q{k}" if slot >= 6 else "kvq.h{k}") if isinstance(it, int) and it == 0 and par == 0 else None)
                        if isinstance(it, int) and it == 0 and par == 0 and slot == 0:
                            norm("n.kvq")
                    for what, c in plan.get(slot, ()):
                        if what == "VT" and tiles:
                            pe.wait_ge(*at(f"masked9.{pp}" if attn and c == 0 else f"vT{c}.{par}", it))
                            if c > 0:
                                pe.wait_ge(*at(f"V{c - 1}.{par}", it))
                            for b in range(QB):
                                mm = nc.tensor.transpose(banks[2][:, b * P:(b + 1) * P], vT1[:, b * P:(b + 1) * P], ident[:, :])
                            mark(mm, pet, f"vturned{c}.{par}", it)
                        elif what == "t" and attn:
                            tr(c)
                        elif what == "v" and attn:
                            pv1(c, it, pp)
                    if attn and slot < QB:
                        scores1(slot, it, pp)

            head1(0, 0, True, False)
            head1(0, 1, True, True)
            with K.loop(pe, 1, HEADS // 2) as it:
                head1(it, 0, True, True)
                head1(it, 1, True, True)
            head1(HEADS // 2, 0, False, True)
            narrow("att_o", KD, h_ops, "att_o.h{k}")
            norm("n.attpost")
            wide_in("f1_in", 44, "n.f1", 9)
            narrow("f1_out", KF, m_ops, "f1_in.mid_end")
            norm("n.f1post")

            def scores2(i, it, par):
                kit = it if par == 0 else it - 1
                if i == 0:
                    pe.wait_ge(*at(f"{L}qT.{par}", kit))
                    pe.wait_ge(*at(f"{L}V.{par}", it))
                if i == 3:
                    pe.wait_ge(*at(f"{L}masked0.{par}", it))
                mm = nc.tensor.matmul(banks[2 + i % 3][:, 0:(i + 1) * P], qT2[0:96, (par * QB + i) * P:(par * QB + i + 1) * P],
                                      kT2[0:96, par * S:par * S + (i + 1) * P], start=True, stop=True)
                mark(mm, pes, f"{L}scores{i}.{par}", it)

            def turn2(i, it, par):
                pe.wait_ge(*at(f"{L}probs{i}.{par}", it))
                if i >= 2:
                    pe.wait_ge(*at(f"{L}PT{i - 2}.{par}", it))
                off = i * (i + 1) // 2
                for kb in range(i + 1):
                    mm = nc.tensor.transpose(banks[5 + i % 2][:, kb * P:(kb + 1) * P],
                                             T(Pr2, par * 10 + off + kb, P), ident[:, :])
                mark(mm, pet, f"{L}turned{i}.{par}", it)

            def pv2(i, it, par):
                pe.wait_ge(*at(f"{L}PT{i}.{par}", it))
                if i == 0 and par == 0 and not (isinstance(it, int) and it == 0):
                    pe.wait_ge(*at(f"{L}merged", it))
                for kb in range(i + 1):
                    mm = nc.tensor.matmul(banks[7][:, i * P:(i + 1) * P], V2[:, par, kb, :],
                                          T(PT2, i % 2 * QB + kb, P),
                                          start=(par == 0 and i == 0 and kb == 0),
                                          stop=(par == 1 and i == QB - 1 and kb == i), skip_group_check=True)
                mark(mm, pev, f"{L}pv{i}.{par}", it)

            def head2(it, par, tiles, attn):
                pp = 1 - par
                up = f"m{l}_up"
                first = isinstance(it, int) and it == 0 and par == 0
                if tiles:
                    product(up, it, 4, 2 * par, KQ, lambda k: (T(cqhi, k), T(cqlo, k)), banks[0], 2)
                if attn:
                    if isinstance(it, int) and it == 0:
                        pe.wait_ge(*at(f"{L}kvT.{pp}", it))
                    else:
                        pe.wait_ge(*at(f"{L}masked3.{1 - pp}", it if pp == 0 else it - 1))
                    for b in range(QB):
                        mm = nc.tensor.transpose(banks[2][:, b * P:(b + 1) * P], T(kvT2, pp * QB + b, P), ident[:, :])
                    mark(mm, pet, f"{L}vturned.{pp}", it)
                    for i in range(3):
                        scores2(i, it, pp)
                if tiles:
                    product(up, it, 4, 2 * par + 1, KKV, lambda k: (T(ckhi, k), T(cklo, k)), banks[1], 2)
                if attn:
                    scores2(3, it, pp)
                    turn2(0, it, pp)
                    turn2(1, it, pp)
                    pv2(0, it, pp)
                    turn2(2, it, pp)
                    pv2(1, it, pp)
                    turn2(3, it, pp)
                    pv2(2, it, pp)
                    pv2(3, it, pp)

            for l in range(2):
                L = f"l{l}."
                norm(f"n.a{l}")
                wide_in(f"a{l}_in", 44, None, 18 if l == 0 else None)
                narrow(f"a{l}_out", KF, m_ops, f"a{l}_in.mid_end")
                norm(f"n.m{l}")
                for j in range(18):
                    product(f"m{l}_in", 0, 18, j, KD, h_ops, banks[j % 4], 4, f"m{l}_in.h{{k}}" if j == 0 else None)
                    if j == 4:
                        norm_sum(f"{L}n.q")
                    if j == 5:
                        norm_bcast(f"{L}n.q")
                    if j == 7:
                        norm_sum(f"{L}n.kv")
                    if j == 8:
                        norm_bcast(f"{L}n.kv")
                norm(f"{L}n.conv")
                head2(0, 0, True, False)
                head2(0, 1, True, True)
                with K.loop(pe, 1, HEADS // 2) as it:
                    head2(it, 0, True, True)
                    head2(it, 1, True, True)
                head2(HEADS // 2, 0, False, True)
                norm(f"{L}n.attn")
                narrow(f"m{l}_o", KD, h_ops, f"m{l}_o.h{{k}}")
                norm(f"n.b{l}")
                wide_in(f"b{l}_in", 44, None, 27 if l == 0 else None)
                narrow(f"b{l}_out", KF, m_ops, f"b{l}_in.mid_end")
            norm("n.final")

        @block.scalar
        def _(act):
            def prep(stage, i, per_slabs, j):
                s0 = BASE[stage][0]
                s = i * per_slabs + (s0 + j + RING)
                act.wait_ge(raw_in[j % RING], raw_value(s0, per_slabs, i, j + RING))
                act.wait_ge(slab_used, s - RING + 1)
                nc.scalar.activation(T(whi, j % RING, SLABW), T(raw, j % RING, SLABW), ACT.Copy).then_inc(w_hi, 1)

            def act_norm(key, dim, dst=None):
                mark(nc.scalar.activation(small[:, 40:41], small[:, 16:17], ACT.Sqrt), actd)
                act.wait_ge(*at(f"{key}.sum"))
                mark(nc.scalar.activation(small[:, 8:12], STAT[:, 0:QB], ACT.Sqrt, bias=small[:, 16:17],
                                          scale=1.0 / dim), actd, f"{key}.root")
                act.wait_ge(*at(f"{key}.bcast"))
                mark(nc.scalar.activation((bc if dst is None else dst)[:, :], BCAST[:, :], ACT.Copy), actd, f"{key}.bc")

            def narrow(stage, spt, src):
                with K.loop(act, 0, 2) as i:
                    for j in range(4):
                        for m in range(spt):
                            prep(stage, i, 4 * spt, j * spt + m)
                        act.wait_ge(*at(f"{stage}.y{j}", i))
                        mark(nc.scalar.activation(tmp[j % 2][:, 0:S], T(src, i * 4 + j), ACT.Square),
                             actd, f"{stage}.sq{j}", i)

            def residual(key, gname, gj, g2=None):
                for k in range(KD):
                    act.wait_ge(*at(f"{key}.x{k}"))
                    mark(nc.scalar.activation(T(hhi, k), T(x, k), ACT.Copy, scale=col(gname, gj + k)), actd, f"{key}.hi{k}")
                    if g2:
                        mark(nc.scalar.activation(T(qhi, k), T(x, k), ACT.Copy, scale=col(g2[0], g2[1] + k)), actd, f"{key}.qhi{k}")
                for k in range(KD):
                    if k >= 2:
                        act.wait_ge(*at(f"{key}.add{k - 2}"))
                    mark(nc.scalar.activation(tmp[k % 2][:, 0:S], T(x, k), ACT.Square), actd, f"{key}.sq{k}")

            def ffn_in(stage, l, nkey):
                act_norm(nkey, D)

                def body(i):
                    for q in range(2):
                        for n in range(4):
                            prep(stage, i, 8, 4 * q + n)
                            if n < 2:
                                act.wait_ge(*at(f"{stage}.u{n}.{q}", i))
                                mark(nc.scalar.activation(tmp[2 + n][:, 0:S], tmp[n][:, 2:S + 2], ACT.Identity,
                                                          bias=dcol("ffn_dw_b", i * 4 + (l * 44 + 2 * q + n)),
                                                          scale=dcol("ffn_dw", i * 12 + ((l * 44 + 2 * q + n) * FTAPS + 2))),
                                     actd, f"{stage}.tap{n}.{q}", i)
                        act.wait_ge(*at(f"{stage}.c1.{q}", i))
                        mark(nc.scalar.activation(tmp[3][:, 0:S], tmp[3][:, 0:S], ACT.Silu), actd, f"{stage}.silu.{q}", i)
                        act.wait_ge(*at(f"{stage}.prod.{q}", i))
                        mark(nc.scalar.activation(T(mhi, i * 2 + q), tmp[2][:, 0:S], ACT.Copy), actd, f"{stage}.hi.{q}", i)
                with K.loop(act, 0, 11) as i:
                    body(i)

            act.wait_ge(const_in, 16 * NCONST)
            for j in range(RING):
                act.wait_ge(raw_in[j], 16)
                nc.scalar.activation(T(whi, j, SLABW), T(raw, j, SLABW), ACT.Copy).then_inc(w_hi, 1)
            for k in range(KD):
                if k >= 2:
                    act.wait_ge(*at(f"start.add{k - 2}"))
                mark(nc.scalar.activation(tmp[k % 2][:, 0:S], T(x, k), ACT.Square), actd, f"start.sq{k}")
                mark(nc.scalar.activation(T(hhi, k), T(x, k), ACT.Copy, scale=col("x_mixpre", k)), actd, f"start.hi{k}")
            act.wait_ge(*at("ones"))
            mark(nc.scalar.activation(small[:, 0:KD], col("c", 0, KD), ACT.Silu), actd, "silu_c")
            act_norm("n.cm", D)
            for n in range(4):
                prep("cm_in", 0, 8, n)

            def gate(i, q):
                act.wait_ge(*at(f"cm.g.{q}", i))
                mark(nc.scalar.activation(tmp[1][:, 0:S], tmp[1][:, 0:S], ACT.Sigmoid,
                                          bias=dcol("cm_b_in", i * 4 + (2 * q + 1))), actd, f"cm.sig.{q}", i)
                act.wait_ge(*at(f"cm.u.{q}", i))
                mark(nc.scalar.activation(T(y, i * 2 + q), ucv[q][:, TAPS - 1:TAPS - 1 + S], ACT.Identity,
                                          bias=dcol("cm_dw_b", i * 2 + q),
                                          scale=dcol("cm_dw", i * (2 * TAPS) + (q * TAPS + TAPS - 1))),
                     actd, f"cm.tap.{q}", i)
            with K.loop(act, 0, 3) as i:
                for q in range(2):
                    gate(i, q)
                    for n in range(4):
                        prep("cm_in", i, 8, 4 + 4 * q + n)
            gate(3, 0)
            for n in range(4):
                prep("cm_in", 3, 8, 4 + n)
            gate(3, 1)
            act.wait_ge(*at("ln.mean"))
            mark(nc.scalar.activation(bc[:, :], BCAST[:, :], ACT.Copy, scale=1.0 / D), actd, "ln.mean_bc")
            for k in range(KD):
                act.wait_ge(*at(f"ln.d{k}"))
                if k >= 2:
                    act.wait_ge(*at(f"ln.add{k - 2}"))
                mark(nc.scalar.activation(tmp[k % 2][:, 0:S], T(y, k), ACT.Square), actd, f"ln.sq{k}")
            act_norm("n.ln", D)
            for k in range(KD):
                act.wait_ge(*at(f"ln.t{k}"))
                mark(nc.scalar.activation(T(y, k), T(y, k), ACT.Silu, bias=col("cm_ln_b", k)), actd, f"ln.silu{k}")
                act.wait_ge(*at(f"ln.silu{k}"))
                mark(nc.scalar.activation(T(hhi, k), T(y, k), ACT.Copy), actd, f"ln.hi{k}")
            narrow("cm_out", 2, y)
            act_norm("n.cmpost", D)
            residual("cmpost", "ffnpre", 0)
            ffn_in("f0_in", 0, "n.f0")
            narrow("f0_out", 6, y)
            act_norm("n.f0post", D)
            residual("f0post", "kv_g", 0, ("x_mixpre", KD))

            act.wait_ge(table_in, 16)
            SCALE1 = float(DH) ** -0.5

            def head1(it, par, tiles, attn):
                pp = 1 - par
                copies = {2: [("PT", 0)], 3: [("PT", 1), ("PT", 2)], 4: [("V", 0), ("PT", 3), ("PT", 4)],
                          5: [("V", 1), ("PT", 5), ("PT", 6), ("PT", 7)], 6: [("V", 2)]}
                for slot in range(9):
                    if tiles:
                        for m in range(2):
                            prep("kvq", it, 36, 18 * par + 2 * slot + m)
                    for what, c in copies.get(slot, ()):
                        if what == "V" and tiles:
                            act.wait_ge(*at(f"vturned{c}.{par}", it))
                            mark(nc.scalar.activation(V1[:, par * GROUPS + c, :, :], banks[2][:, :].rearrange("p (b d) -> p b d", b=QB),
                                                      ACT.Copy), actd, f"V{c}.{par}", it)
                        elif what == "PT" and attn:
                            n = len(CHUNKS1[c][1])
                            act.wait_ge(*at(f"turned{c}.{pp}", it))
                            mark(nc.scalar.activation(PT1[:, c % 2 * S:c % 2 * S + n * P], banks[5 + c % 2][:, 0:n * P], ACT.Copy),
                                 actd, f"PT{c}.{pp}", it)
                    if attn and slot < QB:
                        i = slot
                        pr = Pr1[:, i % 2 * 10 * P:(i % 2 * 10 + len(blocks1(i))) * P]
                        act.wait_ge(*at(f"negmax{i}.{pp}", it))
                        mark(nc.scalar.activation(pr, pr, ACT.Exp,
                                                  bias=small[:, 24 + i:25 + i], scale=SCALE1,
                                                  accum_out=small[:, 28 + i:29 + i]), actd, f"exp{i}.{pp}", it)

            act_norm("n.kvq", D)
            head1(0, 0, True, False)
            head1(0, 1, True, True)
            with K.loop(act, 1, HEADS // 2) as it:
                head1(it, 0, True, True)
                head1(it, 1, True, True)
            head1(HEADS // 2, 0, False, True)
            for k in range(KD):
                act.wait_ge(*at("att.last"))
                mark(nc.scalar.activation(T(hhi, k), T(y, k), ACT.Copy), actd, f"att.hi{k}")
            narrow("att_o", 2, y)
            act_norm("n.attpost", D)
            residual("attpost", "ffnpre", KD)
            ffn_in("f1_in", 1, "n.f1")
            act.wait_ge(*at("rope.angle"))
            mark(nc.scalar.activation(tables[64:96, 2 * S:3 * S], tmp[2][64:96, 0:S], ACT.Sin), actd, "rope.sin0")
            act.wait_ge(*at("rope.abs"))
            mark(nc.scalar.activation(tables[64:96, S:2 * S], tmp[3][64:96, 0:S], ACT.Sin, scale=-1.0,
                                      bias=small[64:96, 17:18]), actd, "rope.cos")
            narrow("f1_out", 6, y)
            act_norm("n.f1post", D)
            for k in range(KD):
                act.wait_ge(*at(f"f1post.x{k}"))
                if k >= 2:
                    act.wait_ge(*at(f"f1post.add{k - 2}"))
                mark(nc.scalar.activation(tmp[k % 2][:, 0:S], T(x, k), ACT.Square), actd, f"f1post.sq{k}")

            def modulated(stage, shift):
                for k in range(KD):
                    act.wait_ge(*at(f"{stage}.t{k}"))
                    mark(nc.scalar.activation(T(hhi, k), tmp[k % 4][:, 0:S], ACT.Identity, bias=modc[:, shift + k:shift + k + 1]),
                         actd, f"{stage}.hi{k}")

            def glu(stage):
                with K.loop(act, 0, 11) as i:
                    for q in range(2):
                        for n in range(4):
                            prep(stage, i, 8, 4 * q + n)
                        act.wait_ge(slab_used, i * 8 + (BASE[stage][0] + 4 * q + 4))
                        mark(nc.scalar.activation(tmp[q][:, 0:S], banks[2 * q + 1][:, :], ACT.Silu), actd, f"{stage}.silu.{q}", i)
                        act.wait_ge(*at(f"{stage}.prod.{q}", i))
                        mark(nc.scalar.activation(T(mhi, i * 2 + q), tmp[2 + q][:, 0:S], ACT.Copy), actd, f"{stage}.hi.{q}", i)

            SCALE2 = float(NOPE + ROPE) ** -0.5

            def head2(it, par, tiles, attn):
                pp = 1 - par
                if attn:
                    act.wait_ge(*at(f"{L}vturned.{pp}", it))
                    mark(nc.scalar.activation(V2[:, pp, :, pp * VD:(pp + 1) * VD],
                                              banks[2][:, :].rearrange("p (b d) -> p b d", b=QB)[:, :, VD:2 * VD],
                                              ACT.Copy), actd, f"{L}V.{pp}", it)
                if tiles:
                    prep(f"m{l}_up", it, 4, 2 * par)
                for i in range(QB):
                    if i == QB - 1 and tiles:
                        prep(f"m{l}_up", it, 4, 2 * par + 1)
                    if attn:
                        off = i * (i + 1) // 2
                        act.wait_ge(*at(f"{L}negmax{i}.{pp}", it))
                        pr = Pr2[:, (pp * 10 + off) * P:(pp * 10 + off + i + 1) * P]
                        mark(nc.scalar.activation(pr, pr, ACT.Exp, bias=small[:, 24 + i:25 + i], scale=SCALE2,
                                                  accum_out=small[:, 28 + i:29 + i]), actd, f"{L}exp{i}.{pp}", it)
                if attn:
                    for i in range(QB):
                        act.wait_ge(*at(f"{L}turned{i}.{pp}", it))
                        mark(nc.scalar.activation(PT2[:, i % 2 * S:i % 2 * S + (i + 1) * P], banks[5 + i % 2][:, 0:(i + 1) * P], ACT.Copy),
                             actd, f"{L}PT{i}.{pp}", it)
                if tiles:
                    act.wait_ge(*at(f"{L}kvT.{par}", it))
                    mark(nc.scalar.activation(kT2[0:64, par * S:(par + 1) * S], kvT2[0:64, par * S:(par + 1) * S], ACT.Copy), actd, f"{L}kT.{par}", it)

            for l in range(2):
                L = f"l{l}."
                act_norm(f"n.a{l}", D)
                modulated(f"a{l}_in", l * 72)
                glu(f"a{l}_in")
                narrow(f"a{l}_out", 6, x)
                act_norm(f"n.m{l}", D)
                modulated(f"m{l}_in", l * 72 + 3 * KD)
                st = f"m{l}_in"
                for j in range(18):
                    for m in range(2):
                        prep(st, 0, 36, 2 * j + m)
                    if j < 5:
                        src = T(cq, j) if j < 3 else T(ckv, j - 3)
                        gc = col("q_a", l * KQ + j) if j < 3 else col("kv_a", l * KKV + j - 3)
                        dst = T(cqhi, j) if j < 3 else T(ckhi, j - 3)
                        act.wait_ge(*at(f"{st}.y{j}"))
                        if j >= 2:
                            act.wait_ge(*at(f"{st}.add{j - 2}"))
                        mark(nc.scalar.activation(tmp[j % 2][:, 0:S], src, ACT.Square), actd, f"{st}.sq{j}")
                        mark(nc.scalar.activation(dst, src, ACT.Copy, scale=gc), actd, f"{st}.low{j}")
                    if j == 5:
                        act_norm(f"{L}n.q", Q_RANK, bcq)
                    if j == 8:
                        act_norm(f"{L}n.kv", KV_RANK, bckv)
                    if j >= 6 and (j - 6) % 3 == 2:
                        c = (j - 6) // 3
                        act.wait_ge(*at(f"{st}.v{c}"))
                        mark(nc.scalar.activation(T(conv, c), tmp[2][:, 2:S + 2], ACT.Copy,
                                                  scale=col("conv_w", (l * 4 + c) * FTAPS + 2)), actd, f"{st}.tap{c}")
                        act.wait_ge(*at(f"{st}.conv{c}"))
                        mark(nc.scalar.activation(tmp[3][:, 0:S], T(conv, c), ACT.Square), actd, f"{st}.csq{c}")
                act_norm(f"{L}n.conv", 512)
                for c in range(4):
                    act.wait_ge(*at(f"{L}cn.t{c}"))
                    mark(nc.scalar.activation(T(hhi, 4 + c), T(conv, c), ACT.Copy), actd, f"{L}cn.hi{c}")
                head2(0, 0, True, False)
                head2(0, 1, True, True)
                with K.loop(act, 1, HEADS // 2) as it:
                    head2(it, 0, True, True)
                    head2(it, 1, True, True)
                head2(HEADS // 2, 0, False, True)
                for c in range(4):
                    act.wait_ge(*at(f"{L}am{c}"))
                    if c >= 2:
                        act.wait_ge(*at(f"{L}amadd{c - 2}"))
                    mark(nc.scalar.activation(tmp[c % 2][:, 0:S], T(am, c), ACT.Square), actd, f"{L}amsq{c}")
                act_norm(f"{L}n.attn", 512)
                for c in range(4):
                    act.wait_ge(*at(f"{L}an.t{c}"))
                    mark(nc.scalar.activation(T(hhi, c), T(am, c), ACT.Copy), actd, f"{L}an.hi{c}")
                narrow(f"m{l}_o", 2, x)
                act_norm(f"n.b{l}", D)
                modulated(f"b{l}_in", l * 72 + 6 * KD)
                glu(f"b{l}_in")
                narrow(f"b{l}_out", 6, x)
            act_norm("n.final", D)

        @block.vector
        def _(dve):
            def step(ins, keys=(), it=None, ago=0):
                mark(ins, vec, keys, it, ago)

            def own(back=0):
                dve.wait_ge(*K.last(vec, back))

            def prep(stage, i, per_slabs, j):
                dve.wait_ge(w_hi, i * per_slabs + (BASE[stage][0] + j + RING + 1))
                nc.vector.tensor_tensor(T(wlo, j % RING, SLABW), T(raw, j % RING, SLABW),
                                        T(whi, j % RING, SLABW).bitcast(F32), ALU.subtract).then_inc(w_lo, 1)

            def tile_done(stage, i, per_turn, j):
                s0, _, spt = BASE[stage]
                dve.wait_ge(slab_used, i * (per_turn * spt) + (s0 + (j + 1) * spt))

            def dve_norm(key):
                dve.wait_ge(*at(f"{key}.root"))
                step(nc.vector.reciprocal(small[:, 12:16], small[:, 8:12]), f"{key}.rstd")

            def clear_acc():
                step(nc.vector.memset(acc[:, :], 0.0))

            def add_acc(src, after, keys=(), it=None):
                dve.wait_ge(*after)
                own()
                step(nc.vector.tensor_tensor(acc[:, :], acc[:, :], src, ALU.add), keys, it)

            def split(dst, src, g, hi, after, keys):
                dve.wait_ge(*after)
                step(nc.vector.scalar_tensor_tensor(dst, src, g, hi.bitcast(F32), ALU.mult, ALU.subtract), keys)

            def narrow(stage, spt, evac, nkey):
                clear_acc()
                with K.loop(dve, 0, 2) as i:
                    for j in range(4):
                        for m in range(spt):
                            prep(stage, i, 4 * spt, j * spt + m)
                        tile_done(stage, i, 4, j)
                        step(evac(banks[j][:, :], i * 4 + j), (f"{stage}.y{j}", f"{stage}.read{j}"), i)
                        add_acc(tmp[j % 2][:, 0:S], at(f"{stage}.sq{j}", i), (), i)
                K.note(f"{nkey}.acc", vec)
                dve_norm(nkey)

            def post(key, gname, gj, nkey, g1=None, g2=None, nxt=None):
                dve.wait_ge(*at(f"n.{key}.bc"))
                clear_acc()

                def rest(k):
                    if g1:
                        split(T(hlo, k), T(x, k), col(g1[0], g1[1] + k), T(hhi, k), at(f"{key}.hi{k}"), f"{nxt}.h{k}")
                    if g2:
                        split(T(qlo, k), T(x, k), col(g2[0], g2[1] + k), T(qhi, k), at(f"{key}.qhi{k}"), f"kvq.q{k}")
                    if not g1:
                        add_acc(tmp[k % 2][:, 0:S], at(f"{key}.sq{k}"), f"{key}.add{k}")
                for k in range(KD):
                    t = tmp[2 + k % 2][:, 0:S]
                    step(nc.vector.scalar_tensor_tensor(t, T(y, k), col(gname, gj + k), bc[:, :], ALU.mult, ALU.mult))
                    own()
                    step(nc.vector.tensor_tensor(T(x, k), T(x, k), t, ALU.add), f"{key}.x{k}")
                    if k >= 1 and nkey:
                        rest(k - 1)
                if g1:
                    rest(KD - 1)
                    for k in range(KD):
                        add_acc(tmp[k % 2][:, 0:S], at(f"{key}.sq{k}"), f"{key}.add{k}")
                    K.note(f"{nkey}.acc", vec)
                elif nkey:
                    rest(KD - 1)
                    K.note(f"{nkey}.acc", vec)

            def ffn_in(stage, l, nkey, ada0):
                dve_norm(nkey)
                for n in range(2):
                    step(nc.vector.memset(tmp[n][:, 0:2], 0.0))
                dve.wait_ge(*at(f"{nkey}.bc"))

                def body(i):
                    for q in range(2):
                        for n in range(2):
                            j = 2 * q + n
                            prep(stage, i, 8, 4 * q + n)
                            tile_done(stage, i, 4, j)
                            own()
                            step(nc.vector.tensor_tensor(tmp[n][:, 2:S + 2], banks[j][:, :], bc[:, :], ALU.mult),
                                 (f"{stage}.read{j}", f"{stage}.u{n}.{q}"), i)
                        prep(stage, i, 8, 4 * q + 2)
                        for tap in (1, 0):
                            for n in range(2):
                                if tap == 1:
                                    dve.wait_ge(*at(f"{stage}.tap{n}.{q}", i))
                                else:
                                    own(1)
                                c = (l * 44 + 2 * q + n) * FTAPS + tap
                                step(nc.vector.scalar_tensor_tensor(tmp[2 + n][:, 0:S], tmp[n][:, tap:tap + S],
                                                                    dcol("ffn_dw", i * 12 + c), tmp[2 + n][:, 0:S],
                                                                    ALU.mult, ALU.add), () if tap else f"{stage}.c{n}.{q}", i)
                        prep(stage, i, 8, 4 * q + 3)
                        dve.wait_ge(*at(f"{stage}.silu.{q}", i))
                        step(nc.vector.tensor_tensor(tmp[2][:, 0:S], tmp[2][:, 0:S], tmp[3][:, 0:S], ALU.mult),
                             f"{stage}.prod.{q}", i)
                        dve.wait_ge(*at(f"{stage}.hi.{q}", i))
                        step(nc.vector.tensor_tensor(T(mlo, i * 2 + q), tmp[2][:, 0:S], T(mhi, i * 2 + q).bitcast(F32),
                                                     ALU.subtract), (), i)
                with_ada(body, ada0)
                K.note(f"{stage}.mid_end", vec)

            def with_ada(body, ada0):
                body(0)
                with K.loop(dve, 1, 10) as i:
                    body(i)
                    if ada0 is not None:
                        ch = i + (ada0 - 1)
                        dve.wait_ge(ada_sum, ch + 1)
                        nc.vector.tensor_tensor(modc[:, bass.ds(ch * 4, 4)], STAT[:, 8:12],
                                                cols[:, bass.ds(ch * 4 + COLS["b_ada"][0], 4)], ALU.add).then_inc(ada_mod, 1)
                body(10)

            def factors(l):
                dve.wait_ge(ada_mod, ADA_CHUNKS * (l + 1) + 1)
                own()
                for n, g in enumerate(("ffn1_g", "mix_g", "ffn2_g")):
                    m, d = l * 72 + 3 * n * KD, (6 * l + n) * KD
                    step(nc.vector.scalar_tensor_tensor(derived[:, d:d + KD], modc[:, m + KD:m + 2 * KD], 1.0,
                                                        col(g, l * KD, KD), ALU.add, ALU.mult))
                    half = 1.0 if n == 1 else 0.5
                    step(nc.vector.tensor_scalar(derived[:, d + 3 * KD:d + 4 * KD], modc[:, m + 2 * KD:m + 3 * KD], half, half,
                                                 ALU.mult, ALU.add))

            R = slice(64, 96)

            step(nc.vector.memset(ones[:, :], 1.0))
            step(nc.vector.memset(small[:, 17:18], float(np.pi / 2)))
            nc.vector.memset(small[:, 41:42], 0.0).then_inc(ada_mod, 1)
            step(nc.vector.memset(small[:, 16:17], EPS), "ones")
            clear_acc()
            for j in range(RING):
                dve.wait_ge(w_hi, j + 1)
                nc.vector.tensor_tensor(T(wlo, j, SLABW), T(raw, j, SLABW), T(whi, j, SLABW).bitcast(F32),
                                        ALU.subtract).then_inc(w_lo, 1)
            for k in range(KD):
                split(T(hlo, k), T(x, k), col("x_mixpre", k), T(hhi, k), at(f"start.hi{k}"), f"cm_in.h{k}")
                add_acc(tmp[k % 2][:, 0:S], at(f"start.sq{k}"), f"start.add{k}")
            K.note("n.cm.acc", vec)

            dve_norm("n.cm")
            step(nc.vector.memset(ucv[0][:, 0:TAPS - 1], 0.0))
            for n in range(4):
                prep("cm_in", 0, 8, n)
            dve.wait_ge(*at("n.cm.bc"))

            def add_taps(i, q, ago=0):
                yt = T(y, i * 2 + q)
                dve.wait_ge(taps_done, i * 2 + (q + 1))
                own()
                step(nc.vector.tensor_tensor(yt, yt, banks[4 + q][:, :], ALU.add), f"cm.sum.{q}", i, ago)
                own()
                step(nc.vector.tensor_tensor(acc[:, :], acc[:, :], yt, ALU.add), (), i)

            def gated_taps(i, q, ahead):
                for n in range(2):
                    j = 2 * q + n
                    tile_done("cm_in", i, 4, j)
                    step(nc.vector.tensor_tensor(tmp[n][:, 0:S], banks[j][:, :], bc[:, :], ALU.mult),
                         (f"cm_in.read{j}", f"cm.{'ag'[n]}.{q}"), i)
                dve.wait_ge(*at(f"cm.sig.{q}", i))
                if not (isinstance(i, int) and i == 0):
                    dve.wait_ge(taps_done, i * 2 + (q - 1))
                own()
                step(nc.vector.scalar_tensor_tensor(ucv[q][:, TAPS - 1:TAPS - 1 + S], tmp[0][:, 0:S],
                                                    dcol("cm_b_in", i * 4 + 2 * q), tmp[1][:, 0:S], ALU.add, ALU.mult),
                     f"cm.u.{q}", i)
                dve.wait_ge(*at(f"cm.tap.{q}", i))
                yt = T(y, i * 2 + q)
                for tap in range(TAPS_PE, TAPS - 1):
                    own()
                    step(nc.vector.scalar_tensor_tensor(yt, ucv[q][:, tap:tap + S],
                                                        dcol("cm_dw", i * (2 * TAPS) + (q * TAPS + tap)), yt,
                                                        ALU.mult, ALU.add), (), i)
                    n, rest = divmod(tap - TAPS_PE, 4)
                    if ahead and rest == 3:
                        prep("cm_in", i, 8, 4 + 4 * q + n)

            gated_taps(0, 0, True)
            step(nc.vector.memset(ucv[1][:, 0:TAPS - 1], 0.0))
            clear_acc()
            gated_taps(0, 1, True)
            add_taps(0, 0)
            with K.loop(dve, 1, 3) as i:
                gated_taps(i, 0, True)
                add_taps(i - 1, 1, 1)
                gated_taps(i, 1, True)
                add_taps(i, 0)
            gated_taps(3, 0, True)
            add_taps(2, 1)
            gated_taps(3, 1, False)
            add_taps(3, 0)
            add_taps(3, 1)
            K.note("ln.mean_acc", vec)
            dve.wait_ge(*at("ln.mean_bc"))
            own()
            clear_acc()
            for k in range(KD + 1):
                if k < KD:
                    step(nc.vector.tensor_tensor(T(y, k), T(y, k), bc[:, :], ALU.subtract), f"ln.d{k}")
                if k:
                    add_acc(tmp[(k - 1) % 2][:, 0:S], at(f"ln.sq{k - 1}"), f"ln.add{k - 1}")
            K.note("n.ln.acc", vec)
            dve_norm("n.ln")
            dve.wait_ge(*at("n.ln.bc"))
            for k in range(KD + 1):
                if k < KD:
                    step(nc.vector.scalar_tensor_tensor(T(y, k), T(y, k), col("cm_ln_g", k), bc[:, :], ALU.mult, ALU.mult), f"ln.t{k}")
                if k:
                    dve.wait_ge(*at(f"ln.hi{k - 1}"))
                    step(nc.vector.tensor_tensor(T(hlo, k - 1), T(y, k - 1), T(hhi, k - 1).bitcast(F32), ALU.subtract), f"cm_out.h{k - 1}")

            copy = lambda bank, k: nc.vector.tensor_copy(T(y, k), bank)
            narrow("cm_out", 2, lambda bank, k: nc.vector.tensor_scalar(T(y, k), bank, dcol("cm_b_out", k), None, ALU.add), "n.cmpost")
            post("cmpost", "mixpost", 0, "n.f0", ("ffnpre", 0), None, "f0_in")
            ffn_in("f0_in", 0, "n.f0", 0)
            narrow("f0_out", 6, copy, "n.f0post")
            post("f0post", "ffnpost", 0, "n.kvq", ("kv_g", 0), ("x_mixpre", KD), "kvq")

            dve_norm("n.kvq")
            dve.wait_ge(*at("n.kvq.bc"))
            dve.wait_ge(table_in, 16)
            SCALE1 = float(DH) ** -0.5

            def head1(it, par, tiles, attn):
                pp = 1 - par
                for slot in range(9):
                    if tiles:
                        j = 9 * par + slot
                        for m in range(2):
                            prep("kvq", it, 36, 2 * j + m)
                        tile_done("kvq", it, 18, j)
                        g = slot % 3
                        if slot < 3:
                            dst, key = T(kT1, par * GROUPS + g), f"kT{g}.{par}"
                        elif slot < 6:
                            dst, key = vT1[:, :], f"vT{g}.{par}"
                            if g:
                                dve.wait_ge(*at(f"vturned{g - 1}.{par}", it))
                            elif par == 1:
                                dve.wait_ge(*at(f"vturned2.0", it))
                            elif not isinstance(it, int):
                                dve.wait_ge(*at(f"vturned2.1", it - 1))
                        else:
                            dst, key = T(qT1, g), f"qT{g}.{par}"
                        step(nc.vector.tensor_tensor(dst, banks[j % 2][:, :], bc[:, :], ALU.mult), (f"kvq.read{j}", key), it)
                    if not attn:
                        continue
                    if 1 <= slot <= QB:
                        i = slot - 1
                        dve.wait_ge(*at(f"exp{i}.{pp}", it))
                        step(nc.vector.reciprocal(small[:, 32 + i:33 + i], small[:, 28 + i:29 + i]), (), it)
                        own()
                        pr = Pr1[:, i % 2 * 10 * P:(i % 2 * 10 + len(blocks1(i))) * P]
                        step(nc.vector.tensor_scalar(pr, pr, small[:, 32 + i:33 + i], None, ALU.mult), f"probs{i}.{pp}", it)
                    if slot < QB:
                        i, at_block = slot, 0
                        for g in range(GROUPS):
                            nb = min(i, 1) + 1 if g == 0 else i + 1
                            m0 = (2 - nb) * P if g == 0 else 256 + (g - 1) * S + (QB - nb) * P
                            u = GROUPS * i + g
                            dve.wait_ge(*at(f"scores{u}.{pp}", it))
                            dve.sem_inc(passed, 1)
                            step(nc.vector.tensor_tensor_reduce(
                                Pr1[:, (i % 2 * 10 + at_block) * P:(i % 2 * 10 + at_block + nb) * P],
                                banks[2 + u % 3][:, 0:nb * P], tables[:, m0:m0 + nb * P], 1.0, 3 * NEG,
                                ALU.add, ALU.max, small[:, 36 + g:37 + g]), f"masked{u}.{pp}", it)
                            at_block += nb
                        own()
                        step(nc.vector.tensor_reduce(small[:, 20:21], small[:, 36:39], AX_X, ALU.max), (), it)
                        own()
                        step(nc.vector.tensor_scalar(small[:, 24 + i:25 + i], small[:, 20:21], -SCALE1, None, ALU.mult),
                             f"negmax{i}.{pp}", it)
                    if slot == 6:
                        dve.wait_ge(*at(f"pv7.{pp}", it))
                        step(nc.vector.tensor_copy(T(y, it * 2 + (par - 1)), banks[7][:, :]), f"merged.{pp}", it)

            head1(0, 0, True, False)
            head1(0, 1, True, True)
            with K.loop(dve, 1, HEADS // 2) as it:
                head1(it, 0, True, True)
                head1(it, 1, True, True)
            head1(HEADS // 2, 0, False, True)
            K.note("att.last", vec)
            for k in range(KD):
                dve.wait_ge(*at(f"att.hi{k}"))
                own()
                step(nc.vector.tensor_tensor(T(hlo, k), T(y, k), T(hhi, k).bitcast(F32), ALU.subtract), f"att_o.h{k}")
            narrow("att_o", 2, copy, "n.attpost")
            post("attpost", "mixpost", KD, "n.f1", ("ffnpre", KD), None, "f1_in")
            ffn_in("f1_in", 1, "n.f1", 9)
            dve.wait_ge(pos_in, 32)
            own()
            ang, turns, red = tmp[0][R, 0:S], tmp[1][R, 0:S], tmp[2][R, 0:S]
            step(nc.vector.tensor_copy(ang, tables[R, S:2 * S].bitcast(I32)))
            own()
            step(nc.vector.tensor_scalar(ang, ang, cols[R, COLS["inv_freq"][0]:COLS["inv_freq"][0] + 1], None, ALU.mult))
            own()
            MAGIC = float(1.5 * 2 ** 23)
            step(nc.vector.tensor_scalar(turns, ang, float(1 / (2 * np.pi)), MAGIC, ALU.mult, ALU.add))
            own()
            step(nc.vector.tensor_scalar(turns, turns, MAGIC, None, ALU.subtract))
            c1 = 6.28125
            c2 = float(np.float32(round((2 * np.pi - c1) * 2 ** 20) / 2 ** 20))
            c3 = float(2 * np.pi - c1 - c2)
            src = ang
            for part in (c1, c2, c3):
                own()
                step(nc.vector.scalar_tensor_tensor(red, turns, -part, src, ALU.mult, ALU.add))
                src = red
            own()
            step(nc.vector.tensor_scalar(red, red, float(np.float32(3.1415925)), float(np.float32(-3.1415925)), ALU.min, ALU.max), "rope.angle")
            own()
            step(nc.vector.scalar_tensor_tensor(tmp[3][R, 0:S], red, -1.0, red, ALU.mult, ALU.max), "rope.abs")
            dve.wait_ge(*at("rope.cos"))
            step(nc.vector.tensor_scalar(tables[R, 2 * S:3 * S], tables[R, 2 * S:3 * S],
                                         cols[R, COLS["rope_sign"][0]:COLS["rope_sign"][0] + 1], None, ALU.mult))

            factors(0)
            narrow("f1_out", 6, copy, "n.f1post")
            post("f1post", "ffnpost", KD, "n.a0")

            def modulated(stage, gs, shift):
                for k in range(KD + 1):
                    if k < KD:
                        step(nc.vector.scalar_tensor_tensor(tmp[k % 4][:, 0:S], T(x, k), derived[:, gs + k:gs + k + 1], bc[:, :],
                                                            ALU.mult, ALU.mult), f"{stage}.t{k}")
                    if k:
                        m = k - 1
                        dve.wait_ge(*at(f"{stage}.hi{m}"))
                        own(1 if k < KD else 0)
                        step(nc.vector.scalar_tensor_tensor(T(hlo, m), tmp[m % 4][:, 0:S], modc[:, shift + m:shift + m + 1],
                                                            T(hhi, m).bitcast(F32), ALU.add, ALU.subtract), f"{stage}.h{m}")

            def glu(stage, ada0):
                def body(i):
                    for q in range(2):
                        for n in range(3):
                            prep(stage, i, 8, 4 * q + n)
                        dve.wait_ge(*at(f"{stage}.silu.{q}", i))
                        step(nc.vector.tensor_tensor(tmp[2 + q][:, 0:S], banks[2 * q][:, :], tmp[q][:, 0:S], ALU.mult),
                             (f"{stage}.prod.{q}", f"{stage}.read{2 * q}", f"{stage}.read{2 * q + 1}"), i)
                        prep(stage, i, 8, 4 * q + 3)
                        dve.wait_ge(*at(f"{stage}.hi.{q}", i))
                        step(nc.vector.tensor_tensor(T(mlo, i * 2 + q), tmp[2 + q][:, 0:S], T(mhi, i * 2 + q).bitcast(F32),
                                                     ALU.subtract), (), i)
                with_ada(body, ada0)
                K.note(f"{stage}.mid_end", vec)

            def gated(gate):
                return lambda bank, k: nc.vector.scalar_tensor_tensor(T(x, k), bank, derived[:, bass.ds(k + gate, 1)], T(x, k),
                                                                      ALU.mult, ALU.add)

            SWAP = [(p + 16) % 32 for p in range(32)]

            def rope(t, keys=(), it=None):
                own()
                step(nc.vector.tensor_tensor(tmp[1][R, 0:S], t, tables[R, S:2 * S], ALU.mult), (), it)
                step(nc.vector.stream_shuffle(tmp[3][R, 0:S], t, SWAP), (), it)
                own()
                step(nc.vector.tensor_tensor(tmp[3][R, 0:S], tmp[3][R, 0:S], tables[R, 2 * S:3 * S], ALU.mult), (), it)
                own()
                step(nc.vector.tensor_tensor(t, tmp[1][R, 0:S], tmp[3][R, 0:S], ALU.add), keys, it)

            SCALE2 = float(NOPE + ROPE) ** -0.5

            def head2(it, par, tiles, attn):
                pp = 1 - par
                up = f"m{l}_up"

                def mask(i):
                    off = pp * 10 + i * (i + 1) // 2
                    dve.wait_ge(*at(f"{L}scores{i}.{pp}", it))
                    dve.sem_inc(passed, 1)
                    step(nc.vector.tensor_tensor_reduce(Pr2[:, off * P:(off + i + 1) * P], banks[2 + i % 3][:, 0:(i + 1) * P],
                                                        tables[:, (QB - 1 - i) * P:S], 1.0, 3 * NEG, ALU.add, ALU.max,
                                                        small[:, 36 + i:37 + i]), f"{L}masked{i}.{pp}", it)
                    own()
                    step(nc.vector.tensor_scalar(small[:, 24 + i:25 + i], small[:, 36 + i:37 + i], -SCALE2, None, ALU.mult),
                         f"{L}negmax{i}.{pp}", it)

                def divide(i):
                    off = pp * 10 + i * (i + 1) // 2
                    dve.wait_ge(*at(f"{L}exp{i}.{pp}", it))
                    step(nc.vector.reciprocal(small[:, 32 + i:33 + i], small[:, 28 + i:29 + i]), (), it)
                    own()
                    pr = Pr2[:, off * P:(off + i + 1) * P]
                    step(nc.vector.tensor_scalar(pr, pr, small[:, 32 + i:33 + i], None, ALU.mult), f"{L}probs{i}.{pp}", it)

                if tiles:
                    prep(up, it, 4, 2 * par)
                    tile_done(up, it, 4, 2 * par)
                    step(nc.vector.tensor_tensor(T(qT2, par), banks[0][:, :], bcq[:, :], ALU.mult), f"{up}.read{2 * par}", it)
                if attn:
                    mask(0)
                if tiles:
                    rope(T(qT2, par)[R], f"{L}qT.{par}", it)
                if attn:
                    mask(1)
                    mask(2)
                    divide(0)
                if tiles:
                    prep(up, it, 4, 2 * par + 1)
                    tile_done(up, it, 4, 2 * par + 1)
                    step(nc.vector.tensor_tensor(T(kvT2, par), banks[1][:, :], bckv[:, :], ALU.mult),
                         (f"{up}.read{2 * par + 1}", f"{L}kvT.{par}"), it)
                if attn:
                    divide(1)
                    mask(3)
                    divide(2)
                    divide(3)
                    if pp == 1:
                        dve.wait_ge(*at(f"{L}pv3.1", it))
                        step(nc.vector.tensor_copy(T(am, it - 1), banks[7][:, :]), f"{L}merged", it)

            for l in range(2):
                L = f"l{l}."
                if l == 0:
                    dve_norm("n.a0")
                dve.wait_ge(*at(f"n.a{l}.bc"))
                own()
                modulated(f"a{l}_in", 6 * l * KD, l * 72)
                glu(f"a{l}_in", 18 if l == 0 else None)
                narrow(f"a{l}_out", 6, gated((6 * l + 3) * KD), f"n.m{l}")
                dve.wait_ge(*at(f"n.m{l}.bc"))
                modulated(f"m{l}_in", (6 * l + 1) * KD, l * 72 + 3 * KD)
                st = f"m{l}_in"
                clear_acc()
                step(nc.vector.memset(V2[:, :, :, :], 0.0))
                step(nc.vector.memset(tmp[2][:, 0:2], 0.0))

                def low_rank_rest(j):
                    src, dst, hi = ((T(cq, j), T(cqlo, j), T(cqhi, j)) if j < KQ else
                                    (T(ckv, j - KQ), T(cklo, j - KQ), T(ckhi, j - KQ)))
                    g = col("q_a", l * KQ + j) if j < KQ else col("kv_a", l * KKV + j - KQ)
                    split(dst, src, g, hi, at(f"{st}.low{j}"), ())
                    if j == KQ:
                        dve.wait_ge(*at(f"{L}n.q.sum"))
                        clear_acc()
                    add_acc(tmp[j % 2][:, 0:S], at(f"{st}.sq{j}"), f"{st}.add{j}")
                    if j == KQ - 1:
                        K.note(f"{L}n.q.acc", vec)
                    if j == KQ + KKV - 1:
                        K.note(f"{L}n.kv.acc", vec)

                for j in range(18):
                    for m in range(2):
                        prep(st, 0, 36, 2 * j + m)
                    if j == 5:
                        dve_norm(f"{L}n.q")
                    if j == 8:
                        dve_norm(f"{L}n.kv")
                        clear_acc()
                    tile_done(st, 0, 18, j)
                    bank, rd = banks[j % 4], f"{st}.read{j}"
                    if j < 5:
                        step(nc.vector.tensor_copy(T(cq, j) if j < KQ else T(ckv, j - KQ), bank[:, :]), (rd, f"{st}.y{j}"))
                    elif j == 5:
                        step(nc.vector.tensor_copy(kT2[R, 0:S], bank[R, :]), rd)
                    elif j % 3 == 0:
                        step(nc.vector.tensor_copy(tmp[0][:, 0:S], bank[:, :]), rd)
                    elif j % 3 == 1:
                        step(nc.vector.tensor_copy(tmp[1][:, 0:S], bank[:, :]), rd)
                    else:
                        c = (j - 6) // 3
                        own()
                        step(nc.vector.tensor_tensor(tmp[2][:, 2:S + 2], bank[:, :], tmp[1][:, 0:S], ALU.mult), (rd, f"{st}.v{c}"))
                        if c:
                            add_acc(tmp[3][:, 0:S], at(f"{st}.csq{c - 1}"))
                        dve.wait_ge(*at(f"{st}.tap{c}"))
                        for tap in (1, 0):
                            own()
                            step(nc.vector.scalar_tensor_tensor(T(conv, c), tmp[2][:, tap:tap + S],
                                                                col("conv_w", (l * 4 + c) * FTAPS + tap), T(conv, c),
                                                                ALU.mult, ALU.add))
                        own()
                        step(nc.vector.tensor_tensor(T(conv, c), T(conv, c), tmp[0][:, 0:S], ALU.mult), f"{st}.conv{c}")
                    if 1 <= j <= 5:
                        low_rank_rest(j - 1)
                    if j == 5:
                        rope(kT2[R, 0:S])
                        own()
                        step(nc.vector.tensor_copy(kT2[R, S:2 * S], kT2[R, 0:S]))
                add_acc(tmp[3][:, 0:S], at(f"{st}.csq3"))
                K.note(f"{L}n.conv.acc", vec)
                dve_norm(f"{L}n.conv")
                dve.wait_ge(*at(f"{L}n.conv.bc"))

                def normed(src, gname, key, h0):
                    for c in range(5):
                        if c < 4:
                            step(nc.vector.scalar_tensor_tensor(T(src, c), T(src, c), col(gname, l * 4 + c), bc[:, :],
                                                                ALU.mult, ALU.mult), f"{L}{key}.t{c}")
                        if c:
                            dve.wait_ge(*at(f"{L}{key}.hi{c - 1}"))
                            step(nc.vector.tensor_tensor(T(hlo, h0 + c - 1), T(src, c - 1), T(hhi, h0 + c - 1).bitcast(F32),
                                                         ALU.subtract), f"m{l}_o.h{h0 + c - 1}")
                normed(conv, "cn_g", "cn", 4)
                clear_acc()
                head2(0, 0, True, False)
                head2(0, 1, True, True)
                with K.loop(dve, 1, HEADS // 2) as it:
                    head2(it, 0, True, True)
                    head2(it, 1, True, True)
                head2(HEADS // 2, 0, False, True)
                for c in range(4):
                    K.note(f"{L}am{c}", vec) if c == 0 else K.note(f"{L}am{c}", vec)
                for c in range(4):
                    add_acc(tmp[c % 2][:, 0:S], at(f"{L}amsq{c}"), f"{L}amadd{c}")
                K.note(f"{L}n.attn.acc", vec)
                dve_norm(f"{L}n.attn")
                dve.wait_ge(*at(f"{L}n.attn.bc"))
                normed(am, "an_g", "an", 0)
                narrow(f"m{l}_o", 2, gated((6 * l + 4) * KD), f"n.b{l}")
                dve.wait_ge(*at(f"n.b{l}.bc"))
                modulated(f"b{l}_in", (6 * l + 2) * KD, l * 72 + 6 * KD)
                glu(f"b{l}_in", 27 if l == 0 else None)
                if l == 0:
                    factors(1)
                narrow(f"b{l}_out", 6, gated((6 * l + 5) * KD), "n.a1" if l == 0 else "n.final")
            dve.wait_ge(*at("n.final.bc"))
            for k in range(KD):
                step(nc.vector.scalar_tensor_tensor(T(y, k), T(x, k), col("final_g", k), bc[:, :], ALU.mult, ALU.mult), f"final.y{k}")

        return K.table


def slabs_of(w, tiles, k_tiles):
    per = -(-k_tiles // ST)
    out = np.zeros((len(tiles), per * ST, P, P), np.float32)
    for n, c in enumerate(tiles):
        out[n, :k_tiles] = w[:, c:c + P].reshape(k_tiles, P, P)
    return out.reshape(len(tiles) * per, ST, P, P).transpose(0, 2, 1, 3).reshape(-1, P, SLABW)


def pairs(first, second, n):
    return [c for j in range(n) for c in (first + j * P, second + j * P)]


def columns(v):
    return np.ascontiguousarray(np.asarray(v).reshape(-1, P).T)


def masks():
    q = np.arange(P)[:, None]
    dist = q + (QB - 1) * P - np.arange(S)[None, :]
    m = [np.where((dist >= 0) & (dist <= w) & (dist % d == 0), 0.0, NEG).astype(np.float32)
         for w, d in zip(WINDOWS, DILATIONS)]
    causal = np.where(dist >= 0, 0.0, NEG).astype(np.float32)
    return np.concatenate([m[0][:, 2 * P:], m[1], m[2]], 1), causal


def kernel(**inputs):
    import concourse.bacc as bacc
    from concourse.bass_utils import run_bass_kernel_spmd

    a = {k: np.asarray(v) for k, v in inputs.items()}
    heads = [(half * GROUPS + g) * D + h * P for h in range(HEADS) for half in range(2) for g in range(GROUPS)]
    w = [slabs_of(a["cm_w_in"][0], pairs(0, D, KD), KD), slabs_of(a["cm_w_out"][0], range(0, D, P), KD)]

    def ffn(w_in, w_out, first, second):
        return [slabs_of(w_in, pairs(first, second, KF), KD), slabs_of(w_out, range(0, D, P), KF)]
    w += ffn(a["ffn_w_in"][0], a["ffn_w_out"][0], 0, D_FF)
    kv, q = a["w_kv"], a["w_q"][0]
    kvq = np.concatenate([kv, q], 1)
    w.append(slabs_of(kvq, [c for h in range(HEADS) for c in
                            heads[6 * h:6 * h + 6] + [2 * GROUPS * D + g * D + h * P for g in range(GROUPS)]], KD))
    w.append(slabs_of(a["w_o"][0], range(0, D, P), KD))
    w += ffn(a["ffn_w_in"][1], a["ffn_w_out"][1], 0, D_FF)
    for l in range(2):
        w += ffn(a["ffn1_w_gu_2"][l], a["ffn1_w_down_2"][l], D_FF, 0)
        wi = a["w_in_2"][l]
        low = Q_RANK + KV_RANK
        z = np.zeros((D, NOPE), np.float32)
        kpe = np.concatenate([z, wi[:, low:low + ROPE], z[:, :ROPE]], 1)
        wi = np.concatenate([wi[:, :low], kpe, wi[:, low + ROPE:]], 1)
        c0 = low + P
        w.append(slabs_of(wi, list(range(0, c0, P)) + [c0 + part * 512 + c * P for c in range(4) for part in range(3)], KD))
        uq = np.zeros((Q_RANK, HEADS, P), np.float32)
        uq[:, :, :NOPE + ROPE] = a["w_uq_2"][l].reshape(Q_RANK, HEADS, NOPE + ROPE)
        sq = slabs_of(uq.reshape(Q_RANK, HEADS * P), range(0, HEADS * P, P), KQ)
        skv = slabs_of(a["w_ukv_2"][l], range(0, HEADS * P, P), KKV)
        w.append(np.stack([sq, skv], 1).reshape(-1, P, SLABW))
        w.append(slabs_of(a["w_o_2"][l], range(0, D, P), KD))
        w += ffn(a["ffn2_w_gu_2"][l], a["ffn2_w_down_2"][l], D_FF, 0)
    w.append(np.zeros((RING, P, SLABW), np.float32))
    w = np.concatenate(w)
    assert w.shape[0] == SLABS + RING

    def interleave(v):
        m = v.shape[-1] // P // 2
        return np.stack([v[..., :m * P].reshape(*v.shape[:-1], m, P), v[..., m * P:].reshape(*v.shape[:-1], m, P)], -2)

    def taps(v):
        return v.T.reshape(-1, P, v.shape[0]).transpose(1, 0, 2).reshape(P, -1)

    inv = (1.0 / (10000.0 ** (np.arange(0, ROPE, 2, dtype=np.float32) / ROPE))).astype(np.float32)
    freq, sign = np.zeros((P, 1), np.float32), np.zeros((P, 1), np.float32)
    freq[64:96, 0] = np.concatenate([inv, inv])
    sign[64:96, 0] = np.repeat([-1.0, 1.0], 16)
    ffn_dw = np.concatenate([taps(interleave(a["ffn_dw"][l]).reshape(FTAPS, -1)) for l in range(2)], 1)
    parts = {
        "x_mixpre": columns(a["mix_pre_g"]), "mixpost": columns(a["mix_post_g"]), "ffnpre": columns(a["ffn_pre_g"]),
        "ffnpost": columns(a["ffn_post_g"]), "cm_b_in": columns(interleave(a["cm_b_in"][0])), "cm_dw": taps(a["cm_dw"][0]),
        "cm_dw_b": columns(a["cm_dw_b"]), "cm_ln_g": columns(a["cm_ln_g"]), "cm_ln_b": columns(a["cm_ln_b"]),
        "cm_b_out": columns(a["cm_b_out"]), "kv_g": columns(a["kv_norm_g"]), "ffn_dw": ffn_dw,
        "ffn_dw_b": columns(interleave(a["ffn_dw_b"])), "c": columns(a["c_2"]), "b_ada": columns(a["b_ada_2"]),
        "ffn1_g": columns(a["ffn1_norm_2"]), "mix_g": columns(a["mix_norm_2"]), "q_a": columns(a["q_a_norm_2"]),
        "kv_a": columns(a["kv_a_norm_2"]), "conv_w": np.concatenate([taps(a["conv_w_2"][l]) for l in range(2)], 1),
        "an_g": columns(a["attn_out_norm_2"]), "cn_g": columns(a["conv_out_norm_2"]), "ffn2_g": columns(a["ffn2_norm_2"]),
        "final_g": columns(a["final_norm_2"]), "inv_freq": freq, "rope_sign": sign}
    assert all(parts[n].shape == (P, c) for n, (_, c) in COLS.items()), {n: v.shape for n, v in parts.items()}
    m1, causal = masks()
    arrays = {
        "w": w,
        "ada": np.ascontiguousarray(a["w_ada_2"].reshape(2, KD, P, ADA_CHUNKS, ADA_CHUNK).transpose(0, 3, 1, 2, 4)
                                    ).reshape(-1, P, ADA_CHUNK),
        "cols": np.concatenate([parts[n] for n in COLS], 1),
        "x": np.ascontiguousarray(a["x"][0].T.reshape(KD, P, S).transpose(1, 0, 2)).reshape(P, KD * S),
        "pos": a["positions_2"].reshape(1, S), "ident": np.eye(P, dtype=np.float32), "masks1": m1, "causal": causal,
    }

    def program(known):
        nc = bacc.Bacc("TRN2", target_bir_lowering=False, num_devices=1)
        ins = {n: nc.dram_tensor(f"in_{n}", v.shape, mybir.dt.from_np(v.dtype), kind="ExternalInput").ap() for n, v in arrays.items()}
        out = nc.dram_tensor("result", (P, KD * S), F32, kind="ExternalOutput").ap()
        return nc, build(nc, ins, out, known)

    _, table = program(None)
    nc, _ = program(table)
    r = run_bass_kernel_spmd(nc, [{f"in_{n}": v for n, v in arrays.items()}], core_ids=[0])
    out = r.results[0]["result"].reshape(P, KD, S)
    return np.ascontiguousarray(out.transpose(2, 1, 0)).reshape(1, S, D)
```

```python
from contextlib import ExitStack, contextmanager

import numpy as np

import concourse.bass as bass
from concourse import mybir

F32 = mybir.dt.float32
F32R = mybir.dt.float32r
I32 = mybir.dt.int32
ALU = mybir.AluOpType
ACT = mybir.ActivationFunctionType
AX_X = mybir.AxisListType.X

P = 128
D, S = 1024, 512
KD = D // P
D_FF = 2816
KF = D_FF // P
HEADS, DH = 8, 128
GROUPS = 3
WINDOWS, DILATIONS = (128, 512, 2048), (1, 4, 16)
TAPS, FTAPS = 31, 3
TAPS_PE = 12
Q_RANK, KV_RANK, NOPE, ROPE, VD = 384, 256, 64, 32, 64
KQ, KKV = Q_RANK // P, KV_RANK // P
EPS = 1e-6
NEG = -1e30
RING = 4
ST = 4
SLABW = ST * P
QB = S // P
NMOD = 9
ADA_CHUNK = 512
ADA_CHUNKS = NMOD * D // ADA_CHUNK

STAGES = [("cm_in", 16, 2), ("cm_out", 8, 2), ("f0_in", 44, 2), ("f0_out", 8, 6),
          ("kvq", 72, 2), ("att_o", 8, 2), ("f1_in", 44, 2), ("f1_out", 8, 6)]
for _l in range(2):
    STAGES += [(f"a{_l}_in", 44, 2), (f"a{_l}_out", 8, 6), (f"m{_l}_in", 18, 2), (f"m{_l}_up", 16, 1),
               (f"m{_l}_o", 8, 2), (f"b{_l}_in", 44, 2), (f"b{_l}_out", 8, 6)]
BASE = {}
_s = _t = 0
for _name, _n, _spt in STAGES:
    BASE[_name] = (_s, _t, _spt)
    _s += _n * _spt
    _t += _n
SLABS = _s

COLS = {}
_c = 0
for _name, _n in ([("x_mixpre", 2 * KD), ("mixpost", 2 * KD), ("ffnpre", 2 * KD), ("ffnpost", 2 * KD),
                   ("cm_b_in", 16), ("cm_dw", KD * TAPS), ("cm_dw_b", KD), ("cm_ln_g", KD), ("cm_ln_b", KD),
                   ("cm_b_out", KD), ("kv_g", KD), ("ffn_dw", 2 * 44 * FTAPS), ("ffn_dw_b", 2 * 44),
                   ("c", KD), ("b_ada", 2 * 72), ("ffn1_g", 2 * KD), ("mix_g", 2 * KD), ("q_a", 2 * KQ),
                   ("kv_a", 2 * KKV), ("conv_w", 2 * 4 * FTAPS), ("an_g", 2 * 4), ("cn_g", 2 * 4),
                   ("ffn2_g", 2 * KD), ("final_g", KD), ("inv_freq", 1), ("rope_sign", 1)]):
    COLS[_name] = (_c, _n)
    _c += _n
NCOLS = _c


def blocks1(i):
    return [(g, kb) for g in range(GROUPS) for kb in range(max(0, i - 1) if g == 0 else 0, i + 1)]


CHUNKS1 = [(i, list(enumerate(blocks1(i)))[c:c + 4]) for i in range(QB) for c in range(0, len(blocks1(i)), 4)]


class Signal:

    def __init__(self, handle, name):
        self.handle, self.name, self.n = handle, name, 0


class Counts:

    def __init__(self, known, signals):
        self.known, self.signals = known, signals
        self.table = {"loops": []}
        self.loop_ = None

    def mark(self, ins, sig, keys=(), it=None, ago=0):
        ins.then_inc(sig.handle, 1)
        sig.n += 1
        for key in (keys,) if isinstance(keys, str) else keys:
            if self.loop_ is None:
                named = self.table.setdefault(key, {})
                assert it not in named, key
                named[it] = (sig.name, sig.n)
            else:
                self.loop_["pending"].append((key, sig, sig.n, ago))

    def note(self, key, sig):
        self.table[key] = {None: (sig.name, sig.n)}

    @contextmanager
    def loop(self, eng, start, end):
        before = {s.name: s.n for s in self.signals.values()}
        number = len(self.table["loops"])
        self.table["loops"].append(None)
        with eng.Fori(start, end) as i:
            self.loop_ = {"pending": [], "i": i, "start": start, "number": number}
            yield i
        per = {s.name: s.n - before[s.name] for s in self.signals.values()}
        self.table["loops"][number] = per
        for key, sig, n, ago in self.loop_["pending"]:
            self.table.setdefault(key, {})["loop"] = (sig.name, n + per[sig.name] * (ago - start), per[sig.name])
        for s in self.signals.values():
            s.n = before[s.name] + per[s.name] * (end - start)
        self.loop_ = None

    def last(self, sig, back=0):
        if self.known is None:
            return sig.handle, 1
        if self.loop_ is None:
            return sig.handle, sig.n - back
        per = self.known["loops"][self.loop_["number"]][sig.name]
        return sig.handle, self.loop_["i"] * per + (sig.n - back - per * self.loop_["start"])

    def at(self, key, it=None):
        if self.known is None:
            return next(iter(self.signals.values())).handle, 1
        e = self.known[key]
        if it is None or (isinstance(it, int) and it in e):
            name, n = e[it]
            return self.signals[name].handle, n
        if "loop" not in e:
            name, n = e[None]
            return self.signals[name].handle, n
        name, n, per = e["loop"]
        return self.signals[name].handle, it * per + n


def T(buf, k, w=S):
    if isinstance(k, int):
        return buf[:, k * w:(k + 1) * w]
    return buf[:, bass.ds(k * w, w)]


def build(nc, a, out, known):
    with ExitStack() as ctx:
        def sb(name, shape, dt=F32):
            return ctx.enter_context(nc.sbuf_tensor(name, shape, dt))

        def sem(name):
            return ctx.enter_context(nc.semaphore(name))

        raw = sb("w_raw_ring", [P, RING * SLABW])
        whi = sb("w_hi_ring", [P, RING * SLABW], F32R)
        wlo = sb("w_lo_ring", [P, RING * SLABW], F32R)
        x = sb("x", [P, KD * S])
        hhi = sb("h_hi", [P, KD * S], F32R)
        hlo = sb("h_lo", [P, KD * S], F32R)
        y = sb("y", [P, KD * S])
        cols = sb("cols", [P, NCOLS])
        ident = sb("ident", [P, P])
        ones = sb("ones", [P, 1])
        tables = sb("tables", [P, 3 * S])
        tmp = [sb(f"tmp{j}", [P, S + FTAPS - 1]) for j in range(4)]
        bc = sb("bc", [P, S])
        acc = sb("acc", [P, S])
        small = sb("small", [P, 44])
        modc = sb("mod", [P, 2 * 72])
        derived = sb("mod_derived", [P, 2 * 6 * KD])
        ada_w = sb("ada_w", [P, 2 * ADA_CHUNK])
        ada_acc = sb("ada_acc", [P, ADA_CHUNK])
        ada_full = sb("ada_full", [P, ADA_CHUNK])
        arena_bytes = 2 * KF * S * 4
        arena_base = nc.sbuf_base
        sb("arena", [P, arena_bytes // 4])
        A0 = arena_base
        used = [0]

        def at_arena(name, shape, dt=F32):
            size = int(np.prod(shape[1:])) * 4
            t = nc.alloc_sbuf_tensor_at(name, shape, dt, offset=A0 + used[0])
            used[0] += size
            assert used[0] <= arena_bytes, (name, used[0])
            return t

        mhi = at_arena("mid_hi", [P, KF * S], F32R)
        mlo = at_arena("mid_lo", [P, KF * S], F32R)
        used[0] = 0
        diag = at_arena("tap_diagonals", [P, 2 * TAPS_PE * P])
        ucv = [at_arena(f"gated{q}", [P, S + 32]) for q in range(2)]
        used[0] = 0
        qhi = at_arena("q_in_hi", [P, KD * S], F32R)
        qlo = at_arena("q_in_lo", [P, KD * S], F32R)
        kT1 = at_arena("kT1", [P, 2 * GROUPS * S])
        qT1 = at_arena("qT1", [P, GROUPS * S])
        vT1 = at_arena("vT1", [P, S])
        V1 = at_arena("v1", [P, 2 * GROUPS, QB, P])
        Pr1 = at_arena("probs1", [P, 2 * 10 * P])
        PT1 = at_arena("probsT1", [P, 2 * S])
        used[0] = 0
        cq = at_arena("cq", [P, KQ * S])
        ckv = at_arena("ckv", [P, KKV * S])
        cqhi = at_arena("cq_hi", [P, KQ * S], F32R)
        cqlo = at_arena("cq_lo", [P, KQ * S], F32R)
        ckhi = at_arena("ckv_hi", [P, KKV * S], F32R)
        cklo = at_arena("ckv_lo", [P, KKV * S], F32R)
        bcq = at_arena("bc_q", [P, S])
        bckv = at_arena("bc_kv", [P, S])
        conv = at_arena("conv", [P, 4 * S])
        am = at_arena("attn_out", [P, 4 * S])
        qT2 = at_arena("qT2", [P, 2 * S])
        kT2 = at_arena("kT2", [P, 2 * S])
        kvT2 = at_arena("kvT2", [P, 2 * S])
        V2 = at_arena("v2", [P, 2, QB, P])
        Pr2 = at_arena("probs2", [P, 2 * 10 * P])
        PT2 = at_arena("probsT2", [P, 2 * S])

        banks = [ctx.enter_context(nc.psum_tensor(f"bank{j}", [P, S], F32)) for j in range(8)]
        BCAST, STAT = banks[6], banks[7]

        raw_in = [sem(f"raw_in{j}") for j in range(RING)]
        w_hi = sem("w_hi")
        w_lo = sem("w_lo")
        slab_used = sem("slab_used")
        const_in = sem("const_in")
        table_in = sem("table_in")
        pos_in = sem("pos_in")
        stored = sem("stored")
        passed = sem("passed")
        ada_in = [sem("ada_in0"), sem("ada_in1")]
        diag_ready = sem("diag_ready")
        taps_done = sem("taps_done")
        pool_passed = sem("pool_passed")
        ada_step = sem("ada_step")
        ada_ready = sem("ada_ready")
        ada_sum = sem("ada_sum")
        ada_mod = sem("ada_mod")
        sigs = {n: Signal(sem(n), n) for n in
                ("vec_done", "act_done", "pe_norm", "pe_scores", "pe_turned", "pe_pv", "vec_aside")}
        vec, actd, pen, pes, pet, pev, aside = sigs.values()
        K = Counts(known, sigs)
        mark, at = K.mark, K.at
        block = ctx.enter_context(nc.Block())

        def col(name, j=0, n=1):
            c = COLS[name][0]
            return cols[:, c + j:c + j + n]

        def dcol(name, j):
            c = COLS[name][0]
            return cols[:, bass.ds(j + c, 1)]

        def raw_value(base, per, i, j):
            return i * (per // RING * 16) + (base // RING + j // RING + 1) * 16

        NCONST = 6
        @block.sync
        def _(sp):
            sp.dma_start(cols[:, :], a["cols"]).then_inc(const_in, 16)
            for k in range(4):
                sp.dma_start(T(x, k, 2 * S), T(a["x"], k, 2 * S)).then_inc(const_in, 16)
            sp.dma_start(ident[:, :], a["ident"]).then_inc(const_in, 16)
            for j in range(RING):
                sp.dma_start(T(raw, j, SLABW), a["w"][j]).then_inc(raw_in[j], 16)

            def stream(first, end):
                with sp.Fori(first, end) as i:
                    for j in range(RING):
                        sp.wait_ge(w_lo, i * RING + (j + 1))
                        sp.dma_start(T(raw, j, SLABW), a["w"][i * RING + (RING + j)]).then_inc(raw_in[j], 16)

            sp.dma_start(tables[:, 0:256 + 2 * S], a["masks1"]).then_inc(table_in, 16)
            after_att = BASE["f1_in"][0] // RING
            stream(0, after_att)
            sp.wait_ge(*at("att.last"))
            sp.dma_start(tables[:, 0:S], a["causal"]).then_inc(pos_in, 16)
            sp.dma_start(tables[64:96, S:2 * S].bitcast(I32), a["pos"].to_broadcast([ROPE, S])).then_inc(pos_in, 16)
            stream(after_att, SLABS // RING)
            for k in range(KD):
                sp.wait_ge(*at(f"final.y{k}"))
                sp.dma_start(T(out, k), T(y, k)).then_inc(stored, 16)
            sp.wait_ge(stored, 16 * KD)

        @block.gpsimd
        def _(pool):
            pool.wait_ge(const_in, 16 * NCONST)

            def diagonals(i, q):
                c = COLS["cm_dw"][0]
                w = cols[:, bass.ds(i * (2 * TAPS) + (c + q * TAPS), TAPS_PE)]
                nc.gpsimd.tensor_tensor(
                    diag[:, q * TAPS_PE * P:(q + 1) * TAPS_PE * P].rearrange("p (t f) -> p t f", t=TAPS_PE),
                    ident[:, :].unsqueeze(1).to_broadcast([P, TAPS_PE, P]),
                    w.unsqueeze(2).to_broadcast([P, TAPS_PE, P]), ALU.mult).then_inc(diag_ready, 1)

            for q in range(2):
                diagonals(0, q)
            with pool.Fori(1, 4) as i:
                for q in range(2):
                    pool.wait_ge(taps_done, i * 2 + (q - 1))
                    pool.sem_inc(pool_passed, 1)
                    diagonals(i, q)

            pool.wait_ge(*at("silu_c"))
            steps = 2 * KD - 2

            def load(ch, k):
                pool.dma_start(T(ada_w, k % 2, ADA_CHUNK), a["ada"][ch * KD + k]).then_inc(ada_in[k % 2], 16)

            def chunk(ch, last):
                first = isinstance(ch, int) and ch == 0
                for k in range(KD):
                    if k >= 1:
                        pool.wait_ge(ada_step, ch * steps + (2 * k - 1))
                    elif not first:
                        pool.wait_ge(ada_ready, ch)
                    if k + 1 < KD:
                        load(ch, k + 1)
                    elif not last:
                        load(ch + 1, 0)
                    pool.wait_ge(ada_in[k % 2], ch * (16 * KD // 2) + 16 * (k // 2 + 1))
                    c, w = small[:, k:k + 1].to_broadcast([P, ADA_CHUNK]), T(ada_w, k % 2, ADA_CHUNK)
                    if k == 0:
                        nc.gpsimd.tensor_tensor(ada_acc[:, :], w, c, ALU.mult).then_inc(ada_step, 1)
                        continue
                    nc.gpsimd.tensor_tensor(w, w, c, ALU.mult).then_inc(ada_step, 1)
                    pool.wait_ge(ada_step, ch * steps + 2 * k)
                    if k == KD - 1 and not first:
                        pool.wait_ge(ada_sum, ch)
                    dst, done = (ada_acc, ada_step) if k + 1 < KD else (ada_full, ada_ready)
                    nc.gpsimd.tensor_tensor(dst[:, :], ada_acc[:, :], w, ALU.add).then_inc(done, 1)

            load(0, 0)
            chunk(0, False)
            with pool.Fori(1, 2 * ADA_CHUNKS - 1) as ch:
                chunk(ch, False)
            chunk(2 * ADA_CHUNKS - 1, True)

        @block.tensor
        def _(pe):
            def product(stage, i, per_turn, j, kt, ops, bank, nbanks, ready=None):
                s0, _, spt = BASE[stage]
                sl = spt * j
                s = i * (per_turn * spt) + (s0 + sl)
                if j >= nbanks:
                    pe.wait_ge(*at(f"{stage}.read{j - nbanks}", i))
                elif not isinstance(i, int) or i > 0:
                    pe.wait_ge(*at(f"{stage}.read{j - nbanks + per_turn}", i - 1))
                o = bank[:, :]
                for k in range(kt):
                    slot = (sl + k // ST) % RING
                    if k % ST == 0:
                        pe.wait_ge(w_lo, s + (k // ST + 1))
                    if callable(ready):
                        if k in (0, KF - 2, KF - 1):
                            pe.wait_ge(*ready(k))
                    elif ready is not None:
                        pe.wait_ge(*at(ready.format(k=k)))
                    wh, wl = T(whi, slot * ST + k % ST, P), T(wlo, slot * ST + k % ST, P)
                    hi, lo = ops(k)
                    nc.tensor.matmul(o, wh, hi, start=(k == 0), stop=False)
                    nc.tensor.matmul(o, wh, lo, start=False, stop=False)
                    mm = nc.tensor.matmul(o, wl, hi, start=False, stop=(k == kt - 1))
                    if k % ST == ST - 1 or k == kt - 1:
                        mm.then_inc(slab_used, 1)

            def first_pair(stage, ready):
                s0 = BASE[stage][0]
                pe.wait_ge(w_lo, s0 + RING)
                for k in range(KD):
                    pe.wait_ge(*at(ready.format(k=k)))
                    for j in range(2):
                        slot = 2 * j + k // ST
                        wh, wl = T(whi, slot * ST + k % ST, P), T(wlo, slot * ST + k % ST, P)
                        hi, lo = h_ops(k)
                        nc.tensor.matmul(banks[j][:, :], wh, hi, start=(k == 0), stop=False)
                        nc.tensor.matmul(banks[j][:, :], wh, lo, start=False, stop=False)
                        mm = nc.tensor.matmul(banks[j][:, :], wl, hi, start=False, stop=(k == KD - 1))
                        if j == 0 and k % ST == ST - 1:
                            mm.then_inc(slab_used, 1)
                        elif j == 1 and k == KD - 1:
                            mm.then_inc(slab_used, 2)

            h_ops = lambda k: (T(hhi, k), T(hlo, k))
            m_ops = lambda k: (T(mhi, k), T(mlo, k))
            q_ops = lambda k: (T(qhi, k), T(qlo, k))

            def norm_sum(key):
                pe.wait_ge(*at(f"{key}.acc"))
                for b in range(QB):
                    mm = nc.tensor.matmul(STAT[:, b:b + 1], acc[:, b * P:(b + 1) * P], ones[:, 0:1],
                                          start=True, stop=True)
                mark(mm, pen, f"{key}.sum")

            def norm_bcast(key):
                pe.wait_ge(*at(f"{key}.rstd"))
                for b in range(QB):
                    mm = nc.tensor.matmul(BCAST[:, b * P:(b + 1) * P], small[:, 12 + b:13 + b].to_broadcast([P, P]),
                                          ident[:, :], start=True, stop=True)
                mark(mm, pen, f"{key}.bcast")

            def norm(key):
                norm_sum(key)
                norm_bcast(key)

            def ada(ch):
                pe.wait_ge(ada_ready, ch + 1)
                pe.wait_ge(ada_mod, ch + 1)
                for b in range(4):
                    mm = nc.tensor.matmul(STAT[:, 8 + b:9 + b], ada_full[:, b * P:(b + 1) * P], ones[:, 0:1],
                                          start=True, stop=True)
                mm.then_inc(ada_sum, 1)

            def wide_in(stage, tiles, nkey=None, ada0=None):
                def body(i):
                    first = isinstance(i, int) and i == 0
                    if first:
                        first_pair(stage, f"{stage}.h{{k}}")
                        if nkey:
                            norm(nkey)
                    for j in range(2 if first else 0, 4):
                        product(stage, i, 4, j, KD, h_ops, banks[j], 4)
                body(0)
                if ada0 is None:
                    with K.loop(pe, 1, tiles // 4) as i:
                        body(i)
                else:
                    with K.loop(pe, 1, 10) as i:
                        body(i)
                        ada(i + (ada0 - 1))
                    body(10)

            def down(stage, stage_in):
                turns = KF // 2
                pe.wait_ge(*at(f"{stage_in}.read1", turns - 1))
                narrow(stage, KF, m_ops, lambda k: at(f"{stage_in}.lo.{k % 2}", turns - 1) if k else
                       at(f"{stage_in}.lo.1", turns - 2))

            def narrow(stage, kt, ops, ready=None):
                with K.loop(pe, 0, 2) as i:
                    for j in range(4):
                        product(stage, i, 4, j, kt, ops, banks[j], 4, ready)

            pe.wait_ge(const_in, 16 * NCONST)
            pe.wait_ge(*at("ones"))

            def products(i, q):
                for j in (2 * q, 2 * q + 1):
                    product("cm_in", i, 4, j, KD, h_ops, banks[j], 4)

            def taps(i, q):
                pe.wait_ge(diag_ready, i * 2 + (q + 1))
                pe.wait_ge(*at(f"cm.u.{q}", i))
                if not (isinstance(i, int) and i == 0):
                    pe.wait_ge(*at(f"cm.sum.{q}", i - 1))
                for tap in range(TAPS_PE):
                    mm = nc.tensor.matmul(banks[4 + q][:, :], T(diag, q * TAPS_PE + tap, P), ucv[q][:, tap:tap + S],
                                          start=(tap == 0), stop=(tap == TAPS_PE - 1))
                mm.then_inc(taps_done, 1)

            first_pair("cm_in", "cm_in.h{k}")
            norm("n.cm")
            products(0, 1)
            taps(0, 0)
            with K.loop(pe, 1, 4) as i:
                products(i, 0)
                taps(i - 1, 1)
                products(i, 1)
                taps(i, 0)
            taps(3, 1)
            pe.wait_ge(*at("ln.mean_acc"))
            mark(nc.tensor.matmul(BCAST[:, :], ones[:, 0:1].to_broadcast([P, P]), acc[:, :], start=True, stop=True), pen, "ln.mean")
            norm("n.ln")
            narrow("cm_out", KD, h_ops, "cm_out.h{k}")
            norm("n.cmpost")
            wide_in("f0_in", 44, "n.f0", 0)
            down("f0_out", "f0_in")
            norm("n.f0post")

            def scores1(i, it, par):
                for g in range(GROUPS):
                    u = GROUPS * i + g
                    k0 = max(0, i - 1) if g == 0 else 0
                    if i == 0 and g == 0:
                        pe.wait_ge(*at(f"qT{GROUPS - 1}.{par}", it if par == 0 else it - 1))
                        pe.wait_ge(*at(f"V{GROUPS - 1}.{par}", it if par == 0 else it - 1))
                    if u >= 3:
                        pe.wait_ge(*at(f"masked{u - 3}.{par}", it))
                    mm = nc.tensor.matmul(banks[2 + u % 3][:, 0:(i + 1 - k0) * P], T(qT1, g * QB + i, P),
                                          kT1[:, ((par * GROUPS + g) * QB + k0) * P:((par * GROUPS + g) * QB + i + 1) * P], start=True, stop=True)
                    mark(mm, pes, f"scores{u}.{par}", it)

            def turn(c, it, par, chunks, Pr):
                i, bl = chunks[c]
                pe.wait_ge(*at(f"probs{i}.{par}", it))
                if c >= 2:
                    pe.wait_ge(*at(f"PT{c - 2}.{par}", it))
                for n, (m, _) in enumerate(bl):
                    mm = nc.tensor.transpose(banks[5 + c % 2][:, n * P:(n + 1) * P], Pr(i, m), ident[:, :])
                mark(mm, pet, f"turned{c}.{par}", it)

            def pv1(c, it, par):
                i, bl = CHUNKS1[c]
                pe.wait_ge(*at(f"PT{c}.{par}", it))
                if c == 0 and not (isinstance(it, int) and it == 0):
                    pe.wait_ge(*at(f"merged.{1 - par}", it if par == 0 else it - 1))
                for n, (_, (g, kb)) in enumerate(bl):
                    mm = nc.tensor.matmul(banks[7][:, i * P:(i + 1) * P], V1[:, par * GROUPS + g, kb, :],
                                          T(PT1, c % 2 * QB + n, P), start=(c == 0 and n == 0),
                                          stop=(c == len(CHUNKS1) - 1 and n == len(bl) - 1), skip_group_check=True)
                mark(mm, pev, f"pv{c}.{par}", it)

            def head1(it, par, tiles, attn):
                pp = 1 - par
                prob = lambda i, m: T(Pr1, i % 2 * 10 + m, P)
                tr = lambda c: turn(c, it, pp, CHUNKS1, prob)
                plan = {2: [("t", 0)], 3: [("v", 0), ("t", 1), ("t", 2), ("v", 1)],
                        4: [("v", 2), ("VT", 0), ("t", 3), ("t", 4), ("v", 3)],
                        5: [("v", 4), ("VT", 1), ("t", 5), ("t", 6), ("v", 5), ("t", 7), ("v", 6)],
                        6: [("v", 7), ("VT", 2)]}
                first = isinstance(it, int) and it == 0 and par == 0
                for slot in range(9):
                    if first and slot == 0:
                        first_pair("kvq", "kvq.h{k}")
                        norm("n.kvq")
                    elif tiles and not (first and slot == 1):
                        j = 9 * par + slot
                        product("kvq", it, 18, j, KD, q_ops if slot >= 6 else h_ops, banks[j % 2], 2,
                                "kvq.q{k}" if first and slot == 6 else None)
                    for what, c in plan.get(slot, ()):
                        if what == "VT" and tiles:
                            pe.wait_ge(*at(f"masked9.{pp}" if attn and c == 0 else f"vT{c}.{par}", it))
                            if c > 0:
                                pe.wait_ge(*at(f"V{c - 1}.{par}", it))
                            for b in range(QB):
                                mm = nc.tensor.transpose(banks[2][:, b * P:(b + 1) * P], vT1[:, b * P:(b + 1) * P], ident[:, :])
                            mark(mm, pet, f"vturned{c}.{par}", it)
                        elif what == "t" and attn:
                            tr(c)
                        elif what == "v" and attn:
                            pv1(c, it, pp)
                    if attn and slot < QB:
                        scores1(slot, it, pp)

            head1(0, 0, True, False)
            head1(0, 1, True, True)
            with K.loop(pe, 1, HEADS // 2) as it:
                head1(it, 0, True, True)
                head1(it, 1, True, True)
            head1(HEADS // 2, 0, False, True)
            narrow("att_o", KD, h_ops, "att_o.h{k}")
            norm("n.attpost")
            wide_in("f1_in", 44, "n.f1", 9)
            down("f1_out", "f1_in")
            norm("n.f1post")

            def scores2(i, it, par):
                if i == 0:
                    pe.wait_ge(*at(f"{L}kT.{par}", it if par == 0 else it - 1))
                if i == 2:
                    pe.wait_ge(*at(f"{L}V.{par}", it))
                if i == 3:
                    pe.wait_ge(*at(f"{L}masked0.{par}", it))
                mm = nc.tensor.matmul(banks[2 + (i + 1) % 3][:, 0:(i + 1) * P], qT2[0:96, (par * QB + i) * P:(par * QB + i + 1) * P],
                                      kT2[0:96, par * S:par * S + (i + 1) * P], start=True, stop=True)
                mark(mm, pes, f"{L}scores{i}.{par}", it)

            def turn2(i, it, par):
                pe.wait_ge(*at(f"{L}probs{i}.{par}", it - 1 if par == 0 else it))
                if i >= 2:
                    pe.wait_ge(*at(f"{L}PT{i - 2}.{par}", it))
                off = i * (i + 1) // 2
                for kb in range(i + 1):
                    mm = nc.tensor.transpose(banks[5 + i % 2][:, kb * P:(kb + 1) * P],
                                             T(Pr2, par * 10 + off + kb, P), ident[:, :])
                mark(mm, pet, f"{L}turned{i}.{par}", it)

            def pv2(i, it, par):
                pe.wait_ge(*at(f"{L}PT{i}.{par}", it))
                if i == 0 and par == 0:
                    pe.wait_ge(*at(f"{L}merged", it - 1))
                for kb in range(i + 1):
                    mm = nc.tensor.matmul(banks[7][:, i * P:(i + 1) * P], V2[:, par, kb, :],
                                          T(PT2, i % 2 * QB + kb, P),
                                          start=(par == 0 and i == 0 and kb == 0),
                                          stop=(par == 1 and i == QB - 1 and kb == i), skip_group_check=True)
                mark(mm, pev, f"{L}pv{i}.{par}", it)

            def head2(it, par, tiles, attn, values):
                pp = 1 - par
                up = f"m{l}_up"
                if values:
                    turn2(0, it, par)
                    turn2(1, it, par)
                    pv2(0, it, par)
                    turn2(2, it, par)
                    pv2(1, it, par)
                if attn:
                    pe.wait_ge(*at(f"{L}kvT.{pp}", it if pp == 0 else it - 1))
                    for b in range(QB):
                        mm = nc.tensor.transpose(banks[2][:, b * P:(b + 1) * P], T(kvT2, pp * QB + b, P), ident[:, :])
                    mark(mm, pet, f"{L}vturned.{pp}", it)
                    scores2(0, it, pp)
                    scores2(1, it, pp)
                if values:
                    turn2(3, it, par)
                    pv2(2, it, par)
                if attn:
                    scores2(2, it, pp)
                if values:
                    pv2(3, it, par)
                if attn:
                    scores2(3, it, pp)
                if tiles:
                    product(up, it, 4, 2 * par, KQ, lambda k: (T(cqhi, k), T(cqlo, k)), banks[0], 2)
                    product(up, it, 4, 2 * par + 1, KKV, lambda k: (T(ckhi, k), T(cklo, k)), banks[1], 2)

            for l in range(2):
                L = f"l{l}."
                norm(f"n.a{l}")
                wide_in(f"a{l}_in", 44, None, 18 if l == 0 else None)
                down(f"a{l}_out", f"a{l}_in")
                norm(f"n.m{l}")
                first_pair(f"m{l}_in", f"m{l}_in.h{{k}}")
                for j in range(2, 18):
                    product(f"m{l}_in", 0, 18, j, KD, h_ops, banks[j % 4], 4)
                    if j == 4:
                        norm_sum(f"{L}n.q")
                    if j == 5:
                        norm_bcast(f"{L}n.q")
                    if j == 7:
                        norm_sum(f"{L}n.kv")
                    if j == 8:
                        norm_bcast(f"{L}n.kv")
                norm(f"{L}n.conv")
                head2(0, 0, True, False, False)
                head2(0, 1, True, True, False)
                with K.loop(pe, 1, HEADS // 2) as it:
                    head2(it, 0, True, True, True)
                    head2(it, 1, True, True, True)
                head2(HEADS // 2, 0, False, True, True)
                head2(HEADS // 2, 1, False, False, True)
                norm(f"{L}n.attn")
                narrow(f"m{l}_o", KD, h_ops, f"m{l}_o.h{{k}}")
                norm(f"n.b{l}")
                wide_in(f"b{l}_in", 44, None, 27 if l == 0 else None)
                down(f"b{l}_out", f"b{l}_in")
            norm("n.final")

        @block.scalar
        def _(act):
            def prep(stage, i, per_slabs, j):
                s0 = BASE[stage][0]
                s = i * per_slabs + (s0 + j + RING)
                act.wait_ge(raw_in[j % RING], raw_value(s0, per_slabs, i, j + RING))
                act.wait_ge(slab_used, s - RING + 1)
                nc.scalar.activation(T(whi, j % RING, SLABW), T(raw, j % RING, SLABW), ACT.Copy).then_inc(w_hi, 1)

            def act_norm(key, dim, dst=None, copy=True):
                mark(nc.scalar.activation(small[:, 40:41], small[:, 16:17], ACT.Sqrt), actd)
                act.wait_ge(*at(f"{key}.sum"))
                mark(nc.scalar.activation(small[:, 8:12], STAT[:, 0:QB], ACT.Sqrt, bias=small[:, 16:17],
                                          scale=1.0 / dim), actd, f"{key}.root")
                if not copy:
                    return
                act.wait_ge(*at(f"{key}.bcast"))
                mark(nc.scalar.activation((bc if dst is None else dst)[:, :], BCAST[:, :], ACT.Copy), actd, f"{key}.bc")

            def narrow(stage, spt, src):
                with K.loop(act, 0, 2) as i:
                    for j in range(4):
                        for m in range(spt):
                            prep(stage, i, 4 * spt, j * spt + m)
                        act.wait_ge(*at(f"{stage}.y{j}", i))
                        mark(nc.scalar.activation(tmp[j % 2][:, 0:S], T(src, i * 4 + j), ACT.Square),
                             actd, f"{stage}.sq{j}", i)

            def residual(key, gname, gj, g2=None):
                for k in range(KD):
                    act.wait_ge(*at(f"{key}.x{k}"))
                    mark(nc.scalar.activation(T(hhi, k), T(x, k), ACT.Copy, scale=col(gname, gj + k)), actd, f"{key}.hi{k}")
                    if g2:
                        mark(nc.scalar.activation(T(qhi, k), T(x, k), ACT.Copy, scale=col(g2[0], g2[1] + k)), actd, f"{key}.qhi{k}")
                for k in range(KD):
                    if k >= 2:
                        act.wait_ge(*at(f"{key}.add{k - 2}"))
                    mark(nc.scalar.activation(tmp[k % 2][:, 0:S], T(x, k), ACT.Square), actd, f"{key}.sq{k}")

            def ffn_in(stage, l, nkey):
                act_norm(nkey, D)

                for n in range(2):
                    prep(stage, 0, 8, n)

                def body(i):
                    for q in range(2):
                        more = not (isinstance(i, int) and i == KF // 2 - 1 and q == 1)
                        for n in range(2):
                            act.wait_ge(*at(f"{stage}.u{n}.{q}", i))
                            mark(nc.scalar.activation(tmp[2 + n][:, 0:S], tmp[n][:, 2:S + 2], ACT.Identity,
                                                      bias=dcol("ffn_dw_b", i * 4 + (l * 44 + 2 * q + n)),
                                                      scale=dcol("ffn_dw", i * 12 + ((l * 44 + 2 * q + n) * FTAPS + 2))),
                                 actd, f"{stage}.tap{n}.{q}", i)
                            prep(stage, i, 8, 4 * q + 2 + n)
                        act.wait_ge(*at(f"{stage}.c1.{q}", i))
                        mark(nc.scalar.activation(tmp[3][:, 0:S], tmp[3][:, 0:S], ACT.Silu), actd, f"{stage}.silu.{q}", i)
                        if more:
                            prep(stage, i, 8, 4 * q + 4)
                        act.wait_ge(*at(f"{stage}.prod.{q}", i))
                        mark(nc.scalar.activation(T(mhi, i * 2 + q), tmp[2][:, 0:S], ACT.Copy), actd, f"{stage}.hi.{q}", i)
                        if more:
                            prep(stage, i, 8, 4 * q + 5)
                with K.loop(act, 0, KF // 2 - 1) as i:
                    body(i)
                body(KF // 2 - 1)

            act.wait_ge(const_in, 16 * NCONST)
            for j in range(RING):
                act.wait_ge(raw_in[j], 16)
                nc.scalar.activation(T(whi, j, SLABW), T(raw, j, SLABW), ACT.Copy).then_inc(w_hi, 1)
            for k in range(KD):
                if k >= 2:
                    act.wait_ge(*at(f"start.add{k - 2}"))
                mark(nc.scalar.activation(tmp[k % 2][:, 0:S], T(x, k), ACT.Square), actd, f"start.sq{k}")
                mark(nc.scalar.activation(T(hhi, k), T(x, k), ACT.Copy, scale=col("x_mixpre", k)), actd, f"start.hi{k}")
            act.wait_ge(*at("ones"))
            mark(nc.scalar.activation(small[:, 0:KD], col("c", 0, KD), ACT.Silu), actd, "silu_c")
            act_norm("n.cm", D)
            for n in range(4):
                prep("cm_in", 0, 8, n)

            def gate(i, q):
                act.wait_ge(*at(f"cm.g.{q}", i))
                mark(nc.scalar.activation(tmp[1][:, 0:S], tmp[1][:, 0:S], ACT.Sigmoid,
                                          bias=dcol("cm_b_in", i * 4 + (2 * q + 1))), actd, f"cm.sig.{q}", i)
                act.wait_ge(*at(f"cm.u.{q}", i))
                mark(nc.scalar.activation(T(y, i * 2 + q), ucv[q][:, TAPS - 1:TAPS - 1 + S], ACT.Identity,
                                          bias=dcol("cm_dw_b", i * 2 + q),
                                          scale=dcol("cm_dw", i * (2 * TAPS) + (q * TAPS + TAPS - 1))),
                     actd, f"cm.tap.{q}", i)
            with K.loop(act, 0, 3) as i:
                for q in range(2):
                    gate(i, q)
                    for n in range(4):
                        prep("cm_in", i, 8, 4 + 4 * q + n)
            gate(3, 0)
            for n in range(4):
                prep("cm_in", 3, 8, 4 + n)
            gate(3, 1)
            act.wait_ge(*at("ln.mean"))
            mark(nc.scalar.activation(bc[:, :], BCAST[:, :], ACT.Copy, scale=1.0 / D), actd, "ln.mean_bc")
            for k in range(KD):
                act.wait_ge(*at(f"ln.d{k}"))
                if k >= 2:
                    act.wait_ge(*at(f"ln.add{k - 2}"))
                mark(nc.scalar.activation(tmp[k % 2][:, 0:S], T(y, k), ACT.Square), actd, f"ln.sq{k}")
            act_norm("n.ln", D)
            for k in range(KD):
                act.wait_ge(*at(f"ln.t{k}"))
                mark(nc.scalar.activation(T(y, k), T(y, k), ACT.Silu, bias=col("cm_ln_b", k)), actd, f"ln.silu{k}")
                act.wait_ge(*at(f"ln.silu{k}"))
                mark(nc.scalar.activation(T(hhi, k), T(y, k), ACT.Copy), actd, f"ln.hi{k}")
            narrow("cm_out", 2, y)
            act_norm("n.cmpost", D)
            residual("cmpost", "ffnpre", 0)
            ffn_in("f0_in", 0, "n.f0")
            narrow("f0_out", 6, y)
            act_norm("n.f0post", D)
            residual("f0post", "kv_g", 0, ("x_mixpre", KD))

            act.wait_ge(table_in, 16)
            SCALE1 = float(DH) ** -0.5

            def head1(it, par, tiles, attn):
                pp = 1 - par
                copies = {2: [("PT", 0)], 3: [("PT", 1), ("PT", 2)], 4: [("V", 0), ("PT", 3), ("PT", 4)],
                          5: [("V", 1), ("PT", 5), ("PT", 6), ("PT", 7)], 6: [("V", 2)]}
                for slot in range(9):
                    if tiles:
                        for m in range(2):
                            prep("kvq", it, 36, 18 * par + 2 * slot + m)
                    for what, c in copies.get(slot, ()):
                        if what == "V" and tiles:
                            act.wait_ge(*at(f"vturned{c}.{par}", it))
                            mark(nc.scalar.activation(V1[:, par * GROUPS + c, :, :], banks[2][:, :].rearrange("p (b d) -> p b d", b=QB),
                                                      ACT.Copy), actd, f"V{c}.{par}", it)
                        elif what == "PT" and attn:
                            n = len(CHUNKS1[c][1])
                            act.wait_ge(*at(f"turned{c}.{pp}", it))
                            mark(nc.scalar.activation(PT1[:, c % 2 * S:c % 2 * S + n * P], banks[5 + c % 2][:, 0:n * P], ACT.Copy),
                                 actd, f"PT{c}.{pp}", it)
                    if attn and slot < QB:
                        i = slot
                        pr = Pr1[:, i % 2 * 10 * P:(i % 2 * 10 + len(blocks1(i))) * P]
                        act.wait_ge(*at(f"negmax{i}.{pp}", it))
                        mark(nc.scalar.activation(pr, pr, ACT.Exp,
                                                  bias=small[:, 24 + i:25 + i], scale=SCALE1,
                                                  accum_out=small[:, 28 + i:29 + i]), actd, f"exp{i}.{pp}", it)

            act_norm("n.kvq", D)
            head1(0, 0, True, False)
            head1(0, 1, True, True)
            with K.loop(act, 1, HEADS // 2) as it:
                head1(it, 0, True, True)
                head1(it, 1, True, True)
            head1(HEADS // 2, 0, False, True)
            for k in range(KD):
                act.wait_ge(*at("att.last"))
                mark(nc.scalar.activation(T(hhi, k), T(y, k), ACT.Copy), actd, f"att.hi{k}")
            narrow("att_o", 2, y)
            act_norm("n.attpost", D)
            residual("attpost", "ffnpre", KD)
            ffn_in("f1_in", 1, "n.f1")
            act.wait_ge(*at("rope.angle"))
            mark(nc.scalar.activation(tables[64:96, 2 * S:3 * S], tmp[2][64:96, 0:S], ACT.Sin), actd, "rope.sin0")
            act.wait_ge(*at("rope.abs"))
            mark(nc.scalar.activation(tables[64:96, S:2 * S], tmp[3][64:96, 0:S], ACT.Sin, scale=-1.0,
                                      bias=small[64:96, 17:18]), actd, "rope.cos")
            narrow("f1_out", 6, y)
            act_norm("n.f1post", D)
            for k in range(KD):
                act.wait_ge(*at(f"f1post.x{k}"))
                if k >= 2:
                    act.wait_ge(*at(f"f1post.add{k - 2}"))
                mark(nc.scalar.activation(tmp[k % 2][:, 0:S], T(x, k), ACT.Square), actd, f"f1post.sq{k}")

            def modulated(stage, shift):
                for k in range(KD):
                    act.wait_ge(*at(f"{stage}.t{k}"))
                    mark(nc.scalar.activation(T(hhi, k), tmp[k % 4][:, 0:S], ACT.Identity, bias=modc[:, shift + k:shift + k + 1]),
                         actd, f"{stage}.hi{k}")

            def glu(stage):
                with K.loop(act, 0, 11) as i:
                    for q in range(2):
                        for n in range(4):
                            prep(stage, i, 8, 4 * q + n)
                        act.wait_ge(slab_used, i * 8 + (BASE[stage][0] + 4 * q + 4))
                        mark(nc.scalar.activation(tmp[q][:, 0:S], banks[2 * q + 1][:, :], ACT.Silu), actd, f"{stage}.silu.{q}", i)
                        act.wait_ge(*at(f"{stage}.prod.{q}", i))
                        mark(nc.scalar.activation(T(mhi, i * 2 + q), tmp[2 + q][:, 0:S], ACT.Copy), actd, f"{stage}.hi.{q}", i)

            SCALE2 = float(NOPE + ROPE) ** -0.5

            def head2(it, par, tiles, attn, values):
                pp = 1 - par

                def turned(i):
                    act.wait_ge(*at(f"{L}turned{i}.{par}", it))
                    mark(nc.scalar.activation(PT2[:, i % 2 * S:i % 2 * S + (i + 1) * P], banks[5 + i % 2][:, 0:(i + 1) * P], ACT.Copy),
                         actd, f"{L}PT{i}.{par}", it)
                if values:
                    for i in range(3):
                        turned(i)
                if attn:
                    act.wait_ge(*at(f"{L}vturned.{pp}", it))
                    mark(nc.scalar.activation(V2[:, pp, :, pp * VD:(pp + 1) * VD],
                                              banks[2][:, :].rearrange("p (b d) -> p b d", b=QB)[:, :, VD:2 * VD],
                                              ACT.Copy), actd, f"{L}V.{pp}", it)
                if values:
                    turned(3)
                if attn:
                    for i in range(QB):
                        off = i * (i + 1) // 2
                        act.wait_ge(*at(f"{L}negmax{i}.{pp}", it))
                        pr = Pr2[:, (pp * 10 + off) * P:(pp * 10 + off + i + 1) * P]
                        mark(nc.scalar.activation(pr, pr, ACT.Exp, bias=small[:, 24 + i:25 + i], scale=SCALE2,
                                                  accum_out=small[:, 28 + i:29 + i]), actd, f"{L}exp{i}.{pp}", it)
                if tiles:
                    for n in range(2):
                        prep(f"m{l}_up", it, 4, 2 * par + n)
                if tiles:
                    act.wait_ge(*at(f"{L}kvT.{par}", it))
                    mark(nc.scalar.activation(kT2[0:64, par * S:(par + 1) * S], kvT2[0:64, par * S:(par + 1) * S], ACT.Copy), actd, f"{L}kT.{par}", it)

            for l in range(2):
                L = f"l{l}."
                act_norm(f"n.a{l}", D, copy=False)
                modulated(f"a{l}_in", l * 72)
                glu(f"a{l}_in")
                narrow(f"a{l}_out", 6, x)
                act_norm(f"n.m{l}", D, copy=False)
                modulated(f"m{l}_in", l * 72 + 3 * KD)
                st = f"m{l}_in"
                for j in range(18):
                    for m in range(2):
                        prep(st, 0, 36, 2 * j + m)
                    if j < 5:
                        src = T(cq, j) if j < 3 else T(ckv, j - 3)
                        gc = col("q_a", l * KQ + j) if j < 3 else col("kv_a", l * KKV + j - 3)
                        dst = T(cqhi, j) if j < 3 else T(ckhi, j - 3)
                        act.wait_ge(*at(f"{st}.y{j}"))
                        if j >= 2:
                            act.wait_ge(*at(f"{st}.add{j - 2}"))
                        mark(nc.scalar.activation(tmp[j % 2][:, 0:S], src, ACT.Square), actd, f"{st}.sq{j}")
                        mark(nc.scalar.activation(dst, src, ACT.Copy, scale=gc), actd, f"{st}.low{j}")
                    if j == 5:
                        act_norm(f"{L}n.q", Q_RANK, bcq)
                    if j == 8:
                        act_norm(f"{L}n.kv", KV_RANK, bckv)
                    if j >= 6 and (j - 6) % 3 == 2:
                        c = (j - 6) // 3
                        act.wait_ge(*at(f"{st}.v{c}"))
                        mark(nc.scalar.activation(T(conv, c), tmp[2][:, 2:S + 2], ACT.Copy,
                                                  scale=col("conv_w", (l * 4 + c) * FTAPS + 2)), actd, f"{st}.tap{c}")
                        act.wait_ge(*at(f"{st}.conv{c}"))
                        mark(nc.scalar.activation(tmp[3][:, 0:S], T(conv, c), ACT.Square), actd, f"{st}.csq{c}")
                act_norm(f"{L}n.conv", 512)
                for c in range(4):
                    act.wait_ge(*at(f"{L}cn.t{c}"))
                    mark(nc.scalar.activation(T(hhi, 4 + c), T(conv, c), ACT.Copy), actd, f"{L}cn.hi{c}")
                head2(0, 0, True, False, False)
                head2(0, 1, True, True, False)
                with K.loop(act, 1, HEADS // 2) as it:
                    head2(it, 0, True, True, True)
                    head2(it, 1, True, True, True)
                head2(HEADS // 2, 0, False, True, True)
                head2(HEADS // 2, 1, False, False, True)
                for c in range(4):
                    act.wait_ge(*at(f"{L}am"))
                    if c >= 2:
                        act.wait_ge(*at(f"{L}amadd{c - 2}"))
                    mark(nc.scalar.activation(tmp[c % 2][:, 0:S], T(am, c), ACT.Square), actd, f"{L}amsq{c}")
                act_norm(f"{L}n.attn", 512)
                for c in range(4):
                    act.wait_ge(*at(f"{L}an.t{c}"))
                    mark(nc.scalar.activation(T(hhi, c), T(am, c), ACT.Copy), actd, f"{L}an.hi{c}")
                narrow(f"m{l}_o", 2, x)
                act_norm(f"n.b{l}", D, copy=False)
                modulated(f"b{l}_in", l * 72 + 6 * KD)
                glu(f"b{l}_in")
                narrow(f"b{l}_out", 6, x)
            act_norm("n.final", D)

        @block.vector
        def _(dve):
            def step(ins, keys=(), it=None, ago=0):
                mark(ins, vec, keys, it, ago)

            def step_aside(ins, keys=()):
                mark(ins, aside, keys)

            def own_aside():
                dve.wait_ge(*K.last(aside))

            def own(back=0):
                dve.wait_ge(*K.last(vec, back))

            def prep(stage, i, per_slabs, j):
                dve.wait_ge(w_hi, i * per_slabs + (BASE[stage][0] + j + RING + 1))
                nc.vector.tensor_tensor(T(wlo, j % RING, SLABW), T(raw, j % RING, SLABW),
                                        T(whi, j % RING, SLABW).bitcast(F32), ALU.subtract).then_inc(w_lo, 1)

            def tile_done(stage, i, per_turn, j):
                s0, _, spt = BASE[stage]
                dve.wait_ge(slab_used, i * (per_turn * spt) + (s0 + (j + 1) * spt))

            def dve_norm(key):
                dve.wait_ge(*at(f"{key}.root"))
                step(nc.vector.reciprocal(small[:, 12:16], small[:, 8:12]), f"{key}.rstd")

            def clear_acc():
                step(nc.vector.memset(acc[:, :], 0.0))

            def add_acc(src, after, keys=(), it=None):
                dve.wait_ge(*after)
                own()
                step(nc.vector.tensor_tensor(acc[:, :], acc[:, :], src, ALU.add), keys, it)

            def split(dst, src, g, hi, after, keys):
                dve.wait_ge(*after)
                step(nc.vector.scalar_tensor_tensor(dst, src, g, hi.bitcast(F32), ALU.mult, ALU.subtract), keys)

            def narrow(stage, spt, evac, nkey):
                clear_acc()
                with K.loop(dve, 0, 2) as i:
                    for j in range(4):
                        for m in range(spt):
                            prep(stage, i, 4 * spt, j * spt + m)
                        tile_done(stage, i, 4, j)
                        step(evac(banks[j][:, :], i * 4 + j), (f"{stage}.y{j}", f"{stage}.read{j}"), i)
                        add_acc(tmp[j % 2][:, 0:S], at(f"{stage}.sq{j}", i), (), i)
                K.note(f"{nkey}.acc", vec)
                dve_norm(nkey)

            def post(key, gname, gj, nkey, g1=None, g2=None, nxt=None):
                dve.wait_ge(*at(f"n.{key}.bc"))
                clear_acc()

                def rest(k):
                    if g1:
                        split(T(hlo, k), T(x, k), col(g1[0], g1[1] + k), T(hhi, k), at(f"{key}.hi{k}"), f"{nxt}.h{k}")
                    if g2:
                        split(T(qlo, k), T(x, k), col(g2[0], g2[1] + k), T(qhi, k), at(f"{key}.qhi{k}"), f"kvq.q{k}")
                    if not g1:
                        add_acc(tmp[k % 2][:, 0:S], at(f"{key}.sq{k}"), f"{key}.add{k}")
                ahead = 1 if g1 else 0
                for k in range(KD + ahead):
                    if k < KD:
                        t = tmp[k % 4 if g1 else 2 + k % 2][:, 0:S]
                        step(nc.vector.scalar_tensor_tensor(t, T(y, k), col(gname, gj + k), bc[:, :], ALU.mult, ALU.mult))
                    m = k - ahead
                    if m >= 0:
                        own(ahead if k < KD else 0)
                        t = tmp[m % 4 if g1 else 2 + m % 2][:, 0:S]
                        step(nc.vector.tensor_tensor(T(x, m), T(x, m), t, ALU.add), f"{key}.x{m}")
                    if m >= 1 and nkey:
                        rest(m - 1)
                if g1:
                    rest(KD - 1)
                    for k in range(KD):
                        add_acc(tmp[k % 2][:, 0:S], at(f"{key}.sq{k}"), f"{key}.add{k}")
                    K.note(f"{nkey}.acc", vec)
                elif nkey:
                    rest(KD - 1)
                    K.note(f"{nkey}.acc", vec)

            def ffn_in(stage, l, nkey, ada0):
                dve_norm(nkey)
                for n in range(2):
                    step(nc.vector.memset(tmp[n][:, 0:2], 0.0))
                dve.wait_ge(*at(f"{nkey}.bc"))

                for n in range(2):
                    prep(stage, 0, 8, n)

                def body(i):
                    for q in range(2):
                        more = not (isinstance(i, int) and i == KF // 2 - 1 and q == 1)
                        for n in range(2):
                            j = 2 * q + n
                            tile_done(stage, i, 4, j)
                            own()
                            step(nc.vector.tensor_tensor(tmp[n][:, 2:S + 2], banks[j][:, :], bc[:, :], ALU.mult),
                                 (f"{stage}.read{j}", f"{stage}.u{n}.{q}"), i)
                        for tap in (1, 0):
                            prep(stage, i, 8, 4 * q + 3 - tap)
                            for n in range(2):
                                if tap == 1:
                                    dve.wait_ge(*at(f"{stage}.tap{n}.{q}", i))
                                else:
                                    own(1)
                                c = (l * 44 + 2 * q + n) * FTAPS + tap
                                step(nc.vector.scalar_tensor_tensor(tmp[2 + n][:, 0:S], tmp[n][:, tap:tap + S],
                                                                    dcol("ffn_dw", i * 12 + c), tmp[2 + n][:, 0:S],
                                                                    ALU.mult, ALU.add), () if tap else f"{stage}.c{n}.{q}", i)
                        if more:
                            prep(stage, i, 8, 4 * q + 4)
                        dve.wait_ge(*at(f"{stage}.silu.{q}", i))
                        step(nc.vector.tensor_tensor(tmp[2][:, 0:S], tmp[2][:, 0:S], tmp[3][:, 0:S], ALU.mult),
                             f"{stage}.prod.{q}", i)
                        if more:
                            prep(stage, i, 8, 4 * q + 5)
                        dve.wait_ge(*at(f"{stage}.hi.{q}", i))
                        step(nc.vector.tensor_tensor(T(mlo, i * 2 + q), tmp[2][:, 0:S], T(mhi, i * 2 + q).bitcast(F32),
                                                     ALU.subtract), f"{stage}.lo.{q}", i)
                with_ada(body, ada0)

            def with_ada(body, ada0):
                body(0)
                with K.loop(dve, 1, 10) as i:
                    body(i)
                    if ada0 is not None:
                        ch = i + (ada0 - 1)
                        dve.wait_ge(ada_sum, ch + 1)
                        nc.vector.tensor_tensor(modc[:, bass.ds(ch * 4, 4)], STAT[:, 8:12],
                                                cols[:, bass.ds(ch * 4 + COLS["b_ada"][0], 4)], ALU.add).then_inc(ada_mod, 1)
                body(10)

            def factors(l):
                dve.wait_ge(ada_mod, ADA_CHUNKS * (l + 1) + 1)
                for n, g in enumerate(("ffn1_g", "mix_g", "ffn2_g")):
                    m, d = l * 72 + 3 * n * KD, (6 * l + n) * KD
                    step_aside(nc.vector.scalar_tensor_tensor(derived[:, d:d + KD], modc[:, m + KD:m + 2 * KD], 1.0,
                                                        col(g, l * KD, KD), ALU.add, ALU.mult))
                    half = 1.0 if n == 1 else 0.5
                    step_aside(nc.vector.tensor_scalar(derived[:, d + 3 * KD:d + 4 * KD], modc[:, m + 2 * KD:m + 3 * KD], half, half,
                                                 ALU.mult, ALU.add))

            R = slice(64, 96)

            step(nc.vector.memset(ones[:, :], 1.0))
            step(nc.vector.memset(small[:, 17:18], float(np.pi / 2)))
            nc.vector.memset(small[:, 41:42], 0.0).then_inc(ada_mod, 1)
            step(nc.vector.memset(small[:, 16:17], EPS), "ones")
            clear_acc()
            for j in range(RING):
                dve.wait_ge(w_hi, j + 1)
                nc.vector.tensor_tensor(T(wlo, j, SLABW), T(raw, j, SLABW), T(whi, j, SLABW).bitcast(F32),
                                        ALU.subtract).then_inc(w_lo, 1)
            for k in range(KD):
                split(T(hlo, k), T(x, k), col("x_mixpre", k), T(hhi, k), at(f"start.hi{k}"), f"cm_in.h{k}")
                add_acc(tmp[k % 2][:, 0:S], at(f"start.sq{k}"), f"start.add{k}")
            K.note("n.cm.acc", vec)

            dve_norm("n.cm")
            step(nc.vector.memset(ucv[0][:, 0:TAPS - 1], 0.0))
            for n in range(4):
                prep("cm_in", 0, 8, n)
            dve.wait_ge(*at("n.cm.bc"))

            def add_taps(i, q, ago=0):
                yt = T(y, i * 2 + q)
                dve.wait_ge(taps_done, i * 2 + (q + 1))
                own()
                step(nc.vector.tensor_tensor(yt, yt, banks[4 + q][:, :], ALU.add), f"cm.sum.{q}", i, ago)
                own()
                step(nc.vector.tensor_tensor(acc[:, :], acc[:, :], yt, ALU.add), (), i)

            def gated_taps(i, q, ahead):
                for n in range(2):
                    j = 2 * q + n
                    tile_done("cm_in", i, 4, j)
                    step(nc.vector.tensor_tensor(tmp[n][:, 0:S], banks[j][:, :], bc[:, :], ALU.mult),
                         (f"cm_in.read{j}", f"cm.{'ag'[n]}.{q}"), i)
                dve.wait_ge(*at(f"cm.sig.{q}", i))
                if not (isinstance(i, int) and i == 0):
                    dve.wait_ge(taps_done, i * 2 + (q - 1))
                own()
                step(nc.vector.scalar_tensor_tensor(ucv[q][:, TAPS - 1:TAPS - 1 + S], tmp[0][:, 0:S],
                                                    dcol("cm_b_in", i * 4 + 2 * q), tmp[1][:, 0:S], ALU.add, ALU.mult),
                     f"cm.u.{q}", i)
                dve.wait_ge(*at(f"cm.tap.{q}", i))
                yt = T(y, i * 2 + q)
                for tap in range(TAPS_PE, TAPS - 1):
                    own()
                    step(nc.vector.scalar_tensor_tensor(yt, ucv[q][:, tap:tap + S],
                                                        dcol("cm_dw", i * (2 * TAPS) + (q * TAPS + tap)), yt,
                                                        ALU.mult, ALU.add), (), i)
                    n, rest = divmod(tap - TAPS_PE, 4)
                    if ahead and rest == 3:
                        prep("cm_in", i, 8, 4 + 4 * q + n)

            gated_taps(0, 0, True)
            step(nc.vector.memset(ucv[1][:, 0:TAPS - 1], 0.0))
            clear_acc()
            gated_taps(0, 1, True)
            add_taps(0, 0)
            with K.loop(dve, 1, 3) as i:
                gated_taps(i, 0, True)
                add_taps(i - 1, 1, 1)
                gated_taps(i, 1, True)
                add_taps(i, 0)
            gated_taps(3, 0, True)
            add_taps(2, 1)
            gated_taps(3, 1, False)
            add_taps(3, 0)
            add_taps(3, 1)
            K.note("ln.mean_acc", vec)
            dve.wait_ge(*at("ln.mean_bc"))
            own()
            clear_acc()
            for k in range(KD + 1):
                if k < KD:
                    step(nc.vector.tensor_tensor(T(y, k), T(y, k), bc[:, :], ALU.subtract), f"ln.d{k}")
                if k:
                    add_acc(tmp[(k - 1) % 2][:, 0:S], at(f"ln.sq{k - 1}"), f"ln.add{k - 1}")
            K.note("n.ln.acc", vec)
            dve_norm("n.ln")
            dve.wait_ge(*at("n.ln.bc"))
            for k in range(KD + 1):
                if k < KD:
                    step(nc.vector.scalar_tensor_tensor(T(y, k), T(y, k), col("cm_ln_g", k), bc[:, :], ALU.mult, ALU.mult), f"ln.t{k}")
                if k:
                    dve.wait_ge(*at(f"ln.hi{k - 1}"))
                    step(nc.vector.tensor_tensor(T(hlo, k - 1), T(y, k - 1), T(hhi, k - 1).bitcast(F32), ALU.subtract), f"cm_out.h{k - 1}")

            copy = lambda bank, k: nc.vector.tensor_copy(T(y, k), bank)
            narrow("cm_out", 2, lambda bank, k: nc.vector.tensor_scalar(T(y, k), bank, dcol("cm_b_out", k), None, ALU.add), "n.cmpost")
            post("cmpost", "mixpost", 0, "n.f0", ("ffnpre", 0), None, "f0_in")
            ffn_in("f0_in", 0, "n.f0", 0)
            narrow("f0_out", 6, copy, "n.f0post")
            post("f0post", "ffnpost", 0, "n.kvq", ("kv_g", 0), ("x_mixpre", KD), "kvq")

            dve_norm("n.kvq")
            dve.wait_ge(*at("n.kvq.bc"))
            dve.wait_ge(table_in, 16)
            SCALE1 = float(DH) ** -0.5

            def head1(it, par, tiles, attn):
                pp = 1 - par
                for slot in range(9):
                    if tiles:
                        j = 9 * par + slot
                        for m in range(2):
                            prep("kvq", it, 36, 2 * j + m)
                        tile_done("kvq", it, 18, j)
                        g = slot % 3
                        if slot < 3:
                            dst, key = T(kT1, par * GROUPS + g), f"kT{g}.{par}"
                        elif slot < 6:
                            dst, key = vT1[:, :], f"vT{g}.{par}"
                            if g:
                                dve.wait_ge(*at(f"vturned{g - 1}.{par}", it))
                            elif par == 1:
                                dve.wait_ge(*at(f"vturned2.0", it))
                            elif not isinstance(it, int):
                                dve.wait_ge(*at(f"vturned2.1", it - 1))
                        else:
                            dst, key = T(qT1, g), f"qT{g}.{par}"
                        step(nc.vector.tensor_tensor(dst, banks[j % 2][:, :], bc[:, :], ALU.mult), (f"kvq.read{j}", key), it)
                    if not attn:
                        continue
                    if 1 <= slot <= QB:
                        i = slot - 1
                        dve.wait_ge(*at(f"exp{i}.{pp}", it))
                        step(nc.vector.reciprocal(small[:, 32 + i:33 + i], small[:, 28 + i:29 + i]), (), it)
                        own()
                        pr = Pr1[:, i % 2 * 10 * P:(i % 2 * 10 + len(blocks1(i))) * P]
                        step(nc.vector.tensor_scalar(pr, pr, small[:, 32 + i:33 + i], None, ALU.mult), f"probs{i}.{pp}", it)
                    if slot < QB:
                        i, at_block = slot, 0
                        for g in range(GROUPS):
                            nb = min(i, 1) + 1 if g == 0 else i + 1
                            m0 = (2 - nb) * P if g == 0 else 256 + (g - 1) * S + (QB - nb) * P
                            u = GROUPS * i + g
                            dve.wait_ge(*at(f"scores{u}.{pp}", it))
                            dve.sem_inc(passed, 1)
                            step(nc.vector.tensor_tensor_reduce(
                                Pr1[:, (i % 2 * 10 + at_block) * P:(i % 2 * 10 + at_block + nb) * P],
                                banks[2 + u % 3][:, 0:nb * P], tables[:, m0:m0 + nb * P], 1.0, 3 * NEG,
                                ALU.add, ALU.max, small[:, 36 + g:37 + g]), f"masked{u}.{pp}", it)
                            at_block += nb
                        own()
                        step(nc.vector.tensor_reduce(small[:, 20:21], small[:, 36:39], AX_X, ALU.max), (), it)
                        own()
                        step(nc.vector.tensor_scalar(small[:, 24 + i:25 + i], small[:, 20:21], -SCALE1, None, ALU.mult),
                             f"negmax{i}.{pp}", it)
                    if slot == 6:
                        dve.wait_ge(*at(f"pv7.{pp}", it))
                        step(nc.vector.tensor_copy(T(y, it * 2 + (par - 1)), banks[7][:, :]), f"merged.{pp}", it)

            head1(0, 0, True, False)
            head1(0, 1, True, True)
            with K.loop(dve, 1, HEADS // 2) as it:
                head1(it, 0, True, True)
                head1(it, 1, True, True)
            head1(HEADS // 2, 0, False, True)
            K.note("att.last", vec)
            for k in range(KD):
                dve.wait_ge(*at(f"att.hi{k}"))
                own()
                step(nc.vector.tensor_tensor(T(hlo, k), T(y, k), T(hhi, k).bitcast(F32), ALU.subtract), f"att_o.h{k}")
            narrow("att_o", 2, copy, "n.attpost")
            post("attpost", "mixpost", KD, "n.f1", ("ffnpre", KD), None, "f1_in")
            ffn_in("f1_in", 1, "n.f1", 9)
            dve.wait_ge(pos_in, 32)
            own()
            ang, turns, red = tmp[0][R, 0:S], tmp[1][R, 0:S], tmp[2][R, 0:S]
            step_aside(nc.vector.tensor_copy(ang, tables[R, S:2 * S].bitcast(I32)))
            own_aside()
            step_aside(nc.vector.tensor_scalar(ang, ang, cols[R, COLS["inv_freq"][0]:COLS["inv_freq"][0] + 1], None, ALU.mult))
            own_aside()
            MAGIC = float(1.5 * 2 ** 23)
            step_aside(nc.vector.tensor_scalar(turns, ang, float(1 / (2 * np.pi)), MAGIC, ALU.mult, ALU.add))
            own_aside()
            step_aside(nc.vector.tensor_scalar(turns, turns, MAGIC, None, ALU.subtract))
            c1 = 6.28125
            c2 = float(np.float32(round((2 * np.pi - c1) * 2 ** 20) / 2 ** 20))
            c3 = float(2 * np.pi - c1 - c2)
            src = ang
            for part in (c1, c2, c3):
                own_aside()
                step_aside(nc.vector.scalar_tensor_tensor(red, turns, -part, src, ALU.mult, ALU.add))
                src = red
            own_aside()
            step_aside(nc.vector.tensor_scalar(red, red, float(np.float32(3.1415925)), float(np.float32(-3.1415925)), ALU.min, ALU.max), "rope.angle")
            own_aside()
            step_aside(nc.vector.scalar_tensor_tensor(tmp[3][R, 0:S], red, -1.0, red, ALU.mult, ALU.max), "rope.abs")
            dve.wait_ge(*at("rope.cos"))
            step_aside(nc.vector.tensor_scalar(tables[R, 2 * S:3 * S], tables[R, 2 * S:3 * S],
                                         cols[R, COLS["rope_sign"][0]:COLS["rope_sign"][0] + 1], None, ALU.mult))

            factors(0)
            own_aside()
            narrow("f1_out", 6, copy, "n.f1post")
            post("f1post", "ffnpost", KD, "n.a0")

            def modulated(stage, gs, shift):
                for k in range(KD + 1):
                    if k < KD:
                        step(nc.vector.scalar_tensor_tensor(tmp[k % 4][:, 0:S], T(x, k), derived[:, gs + k:gs + k + 1], BCAST[:, :],
                                                            ALU.mult, ALU.mult), f"{stage}.t{k}")
                    if k:
                        m = k - 1
                        dve.wait_ge(*at(f"{stage}.hi{m}"))
                        own(1 if k < KD else 0)
                        step(nc.vector.scalar_tensor_tensor(T(hlo, m), tmp[m % 4][:, 0:S], modc[:, shift + m:shift + m + 1],
                                                            T(hhi, m).bitcast(F32), ALU.add, ALU.subtract), f"{stage}.h{m}")

            def glu(stage, ada0):
                def body(i):
                    for q in range(2):
                        for n in range(3):
                            prep(stage, i, 8, 4 * q + n)
                        dve.wait_ge(*at(f"{stage}.silu.{q}", i))
                        step(nc.vector.tensor_tensor(tmp[2 + q][:, 0:S], banks[2 * q][:, :], tmp[q][:, 0:S], ALU.mult),
                             (f"{stage}.prod.{q}", f"{stage}.read{2 * q}", f"{stage}.read{2 * q + 1}"), i)
                        prep(stage, i, 8, 4 * q + 3)
                        dve.wait_ge(*at(f"{stage}.hi.{q}", i))
                        step(nc.vector.tensor_tensor(T(mlo, i * 2 + q), tmp[2 + q][:, 0:S], T(mhi, i * 2 + q).bitcast(F32),
                                                     ALU.subtract), f"{stage}.lo.{q}", i)
                with_ada(body, ada0)

            def gated(gate):
                return lambda bank, k: nc.vector.scalar_tensor_tensor(T(x, k), bank, derived[:, bass.ds(k + gate, 1)], T(x, k),
                                                                      ALU.mult, ALU.add)

            SWAP = [(p + 16) % 32 for p in range(32)]

            def rope(t, keys=(), it=None):
                own()
                step(nc.vector.tensor_tensor(tmp[1][R, 0:S], t, tables[R, S:2 * S], ALU.mult), (), it)
                step(nc.vector.stream_shuffle(tmp[3][R, 0:S], t, SWAP), (), it)
                own()
                step(nc.vector.tensor_tensor(tmp[3][R, 0:S], tmp[3][R, 0:S], tables[R, 2 * S:3 * S], ALU.mult), (), it)
                own()
                step(nc.vector.tensor_tensor(t, tmp[1][R, 0:S], tmp[3][R, 0:S], ALU.add), keys, it)

            SCALE2 = float(NOPE + ROPE) ** -0.5

            def head2(it, par, tiles, attn, values):
                pp = 1 - par
                up = f"m{l}_up"

                def mask(i):
                    off = pp * 10 + i * (i + 1) // 2
                    dve.wait_ge(*at(f"{L}scores{i}.{pp}", it))
                    dve.sem_inc(passed, 1)
                    step(nc.vector.tensor_tensor_reduce(Pr2[:, off * P:(off + i + 1) * P], banks[2 + (i + 1) % 3][:, 0:(i + 1) * P],
                                                        tables[:, (QB - 1 - i) * P:S], 1.0, 3 * NEG, ALU.add, ALU.max,
                                                        small[:, 36 + i:37 + i]), f"{L}masked{i}.{pp}", it)
                    own()
                    step(nc.vector.tensor_scalar(small[:, 24 + i:25 + i], small[:, 36 + i:37 + i], -SCALE2, None, ALU.mult),
                         f"{L}negmax{i}.{pp}", it)

                def divide(i):
                    off = pp * 10 + i * (i + 1) // 2
                    dve.wait_ge(*at(f"{L}exp{i}.{pp}", it))
                    step(nc.vector.reciprocal(small[:, 32 + i:33 + i], small[:, 28 + i:29 + i]), (), it)
                    own()
                    pr = Pr2[:, off * P:(off + i + 1) * P]
                    step(nc.vector.tensor_scalar(pr, pr, small[:, 32 + i:33 + i], None, ALU.mult), f"{L}probs{i}.{pp}", it)

                if attn:
                    for i in range(QB):
                        mask(i)
                        if i >= 2:
                            divide(i - 2)
                    divide(2)
                    divide(3)
                if tiles:
                    tile_done(up, it, 4, 2 * par)
                    step(nc.vector.tensor_tensor(T(qT2, par), banks[0][:, :], bcq[:, :], ALU.mult), f"{up}.read{2 * par}", it)
                    prep(up, it, 4, 2 * par)
                    rope(T(qT2, par)[R], f"{L}qT.{par}", it)
                    tile_done(up, it, 4, 2 * par + 1)
                    step(nc.vector.tensor_tensor(T(kvT2, par), banks[1][:, :], bckv[:, :], ALU.mult),
                         (f"{up}.read{2 * par + 1}", f"{L}kvT.{par}"), it)
                    prep(up, it, 4, 2 * par + 1)
                if par == 1 and values:
                    dve.wait_ge(*at(f"{L}pv3.1", it))
                    step(nc.vector.tensor_copy(T(am, it - 1), banks[7][:, :]), f"{L}merged", it)
                elif par == 1:
                    clear_acc()

            for l in range(2):
                L = f"l{l}."
                if l == 0:
                    dve_norm("n.a0")
                dve.wait_ge(*at(f"n.a{l}.bcast"))
                modulated(f"a{l}_in", 6 * l * KD, l * 72)
                glu(f"a{l}_in", 18 if l == 0 else None)
                narrow(f"a{l}_out", 6, gated((6 * l + 3) * KD), f"n.m{l}")
                dve.wait_ge(*at(f"n.m{l}.bcast"))
                modulated(f"m{l}_in", (6 * l + 1) * KD, l * 72 + 3 * KD)
                st = f"m{l}_in"
                clear_acc()
                step(nc.vector.memset(V2[:, :, :, :], 0.0))
                step(nc.vector.memset(tmp[2][:, 0:2], 0.0))

                def low_rank_rest(j):
                    src, dst, hi = ((T(cq, j), T(cqlo, j), T(cqhi, j)) if j < KQ else
                                    (T(ckv, j - KQ), T(cklo, j - KQ), T(ckhi, j - KQ)))
                    g = col("q_a", l * KQ + j) if j < KQ else col("kv_a", l * KKV + j - KQ)
                    split(dst, src, g, hi, at(f"{st}.low{j}"), ())
                    if j == KQ:
                        dve.wait_ge(*at(f"{L}n.q.sum"))
                        clear_acc()
                    add_acc(tmp[j % 2][:, 0:S], at(f"{st}.sq{j}"), f"{st}.add{j}")
                    if j == KQ - 1:
                        K.note(f"{L}n.q.acc", vec)
                    if j == KQ + KKV - 1:
                        K.note(f"{L}n.kv.acc", vec)

                for j in range(18):
                    for m in range(2):
                        prep(st, 0, 36, 2 * j + m)
                    if j == 5:
                        dve_norm(f"{L}n.q")
                    if j == 8:
                        dve_norm(f"{L}n.kv")
                        clear_acc()
                    tile_done(st, 0, 18, j)
                    bank, rd = banks[j % 4], f"{st}.read{j}"
                    if j < 5:
                        step(nc.vector.tensor_copy(T(cq, j) if j < KQ else T(ckv, j - KQ), bank[:, :]), (rd, f"{st}.y{j}"))
                    elif j == 5:
                        step(nc.vector.tensor_copy(kT2[R, 0:S], bank[R, :]), rd)
                    elif j % 3 == 0:
                        step(nc.vector.tensor_copy(tmp[0][:, 0:S], bank[:, :]), rd)
                    elif j % 3 == 1:
                        step(nc.vector.tensor_copy(tmp[1][:, 0:S], bank[:, :]), rd)
                    else:
                        c = (j - 6) // 3
                        own()
                        step(nc.vector.tensor_tensor(tmp[2][:, 2:S + 2], bank[:, :], tmp[1][:, 0:S], ALU.mult), (rd, f"{st}.v{c}"))
                        if c:
                            add_acc(tmp[3][:, 0:S], at(f"{st}.csq{c - 1}"))
                        dve.wait_ge(*at(f"{st}.tap{c}"))
                        for tap in (1, 0):
                            own()
                            step(nc.vector.scalar_tensor_tensor(T(conv, c), tmp[2][:, tap:tap + S],
                                                                col("conv_w", (l * 4 + c) * FTAPS + tap), T(conv, c),
                                                                ALU.mult, ALU.add))
                        own()
                        step(nc.vector.tensor_tensor(T(conv, c), T(conv, c), tmp[0][:, 0:S], ALU.mult), f"{st}.conv{c}")
                    if 1 <= j <= 5:
                        low_rank_rest(j - 1)
                    if j == 5:
                        rope(kT2[R, 0:S])
                        own()
                        step(nc.vector.tensor_copy(kT2[R, S:2 * S], kT2[R, 0:S]))
                add_acc(tmp[3][:, 0:S], at(f"{st}.csq3"))
                K.note(f"{L}n.conv.acc", vec)
                dve_norm(f"{L}n.conv")
                dve.wait_ge(*at(f"{L}n.conv.bc"))

                def normed(src, gname, key, h0):
                    for c in range(5):
                        if c < 4:
                            step(nc.vector.scalar_tensor_tensor(T(src, c), T(src, c), col(gname, l * 4 + c), bc[:, :],
                                                                ALU.mult, ALU.mult), f"{L}{key}.t{c}")
                        if c:
                            dve.wait_ge(*at(f"{L}{key}.hi{c - 1}"))
                            step(nc.vector.tensor_tensor(T(hlo, h0 + c - 1), T(src, c - 1), T(hhi, h0 + c - 1).bitcast(F32),
                                                         ALU.subtract), f"m{l}_o.h{h0 + c - 1}")
                normed(conv, "cn_g", "cn", 4)
                head2(0, 0, True, False, False)
                head2(0, 1, True, True, False)
                with K.loop(dve, 1, HEADS // 2) as it:
                    head2(it, 0, True, True, True)
                    head2(it, 1, True, True, True)
                head2(HEADS // 2, 0, False, True, True)
                head2(HEADS // 2, 1, False, False, True)
                K.note(f"{L}am", vec)
                for c in range(4):
                    add_acc(tmp[c % 2][:, 0:S], at(f"{L}amsq{c}"), f"{L}amadd{c}")
                K.note(f"{L}n.attn.acc", vec)
                dve_norm(f"{L}n.attn")
                dve.wait_ge(*at(f"{L}n.attn.bc"))
                normed(am, "an_g", "an", 0)
                narrow(f"m{l}_o", 2, gated((6 * l + 4) * KD), f"n.b{l}")
                dve.wait_ge(*at(f"n.b{l}.bcast"))
                modulated(f"b{l}_in", (6 * l + 2) * KD, l * 72 + 6 * KD)
                glu(f"b{l}_in", 27 if l == 0 else None)
                if l == 0:
                    factors(1)
                    own_aside()
                narrow(f"b{l}_out", 6, gated((6 * l + 5) * KD), "n.a1" if l == 0 else "n.final")
            dve.wait_ge(*at("n.final.bc"))
            for k in range(KD):
                step(nc.vector.scalar_tensor_tensor(T(y, k), T(x, k), col("final_g", k), bc[:, :], ALU.mult, ALU.mult), f"final.y{k}")

        return K.table


def slabs_of(w, tiles, k_tiles):
    per = -(-k_tiles // ST)
    out = np.zeros((len(tiles), per * ST, P, P), np.float32)
    for n, c in enumerate(tiles):
        out[n, :k_tiles] = w[:, c:c + P].reshape(k_tiles, P, P)
    return out.reshape(len(tiles) * per, ST, P, P).transpose(0, 2, 1, 3).reshape(-1, P, SLABW)


def pairs(first, second, n):
    return [c for j in range(n) for c in (first + j * P, second + j * P)]


def columns(v):
    return np.ascontiguousarray(np.asarray(v).reshape(-1, P).T)


def masks():
    q = np.arange(P)[:, None]
    dist = q + (QB - 1) * P - np.arange(S)[None, :]
    m = [np.where((dist >= 0) & (dist <= w) & (dist % d == 0), 0.0, NEG).astype(np.float32)
         for w, d in zip(WINDOWS, DILATIONS)]
    causal = np.where(dist >= 0, 0.0, NEG).astype(np.float32)
    return np.concatenate([m[0][:, 2 * P:], m[1], m[2]], 1), causal


def kernel(**inputs):
    import concourse.bacc as bacc
    from concourse.bass_utils import run_bass_kernel_spmd

    a = {k: np.asarray(v) for k, v in inputs.items()}
    heads = [(half * GROUPS + g) * D + h * P for h in range(HEADS) for half in range(2) for g in range(GROUPS)]
    w = [slabs_of(a["cm_w_in"][0], pairs(0, D, KD), KD), slabs_of(a["cm_w_out"][0], range(0, D, P), KD)]

    def ffn(w_in, w_out, first, second):
        return [slabs_of(w_in, pairs(first, second, KF), KD), slabs_of(w_out, range(0, D, P), KF)]
    w += ffn(a["ffn_w_in"][0], a["ffn_w_out"][0], 0, D_FF)
    kv, q = a["w_kv"], a["w_q"][0]
    kvq = np.concatenate([kv, q], 1)
    w.append(slabs_of(kvq, [c for h in range(HEADS) for c in
                            heads[6 * h:6 * h + 6] + [2 * GROUPS * D + g * D + h * P for g in range(GROUPS)]], KD))
    w.append(slabs_of(a["w_o"][0], range(0, D, P), KD))
    w += ffn(a["ffn_w_in"][1], a["ffn_w_out"][1], 0, D_FF)
    for l in range(2):
        w += ffn(a["ffn1_w_gu_2"][l], a["ffn1_w_down_2"][l], D_FF, 0)
        wi = a["w_in_2"][l]
        low = Q_RANK + KV_RANK
        z = np.zeros((D, NOPE), np.float32)
        kpe = np.concatenate([z, wi[:, low:low + ROPE], z[:, :ROPE]], 1)
        wi = np.concatenate([wi[:, :low], kpe, wi[:, low + ROPE:]], 1)
        c0 = low + P
        w.append(slabs_of(wi, list(range(0, c0, P)) + [c0 + part * 512 + c * P for c in range(4) for part in range(3)], KD))
        uq = np.zeros((Q_RANK, HEADS, P), np.float32)
        uq[:, :, :NOPE + ROPE] = a["w_uq_2"][l].reshape(Q_RANK, HEADS, NOPE + ROPE)
        sq = slabs_of(uq.reshape(Q_RANK, HEADS * P), range(0, HEADS * P, P), KQ)
        skv = slabs_of(a["w_ukv_2"][l], range(0, HEADS * P, P), KKV)
        w.append(np.stack([sq, skv], 1).reshape(-1, P, SLABW))
        w.append(slabs_of(a["w_o_2"][l], range(0, D, P), KD))
        w += ffn(a["ffn2_w_gu_2"][l], a["ffn2_w_down_2"][l], D_FF, 0)
    w.append(np.zeros((RING, P, SLABW), np.float32))
    w = np.concatenate(w)
    assert w.shape[0] == SLABS + RING

    def interleave(v):
        m = v.shape[-1] // P // 2
        return np.stack([v[..., :m * P].reshape(*v.shape[:-1], m, P), v[..., m * P:].reshape(*v.shape[:-1], m, P)], -2)

    def taps(v):
        return v.T.reshape(-1, P, v.shape[0]).transpose(1, 0, 2).reshape(P, -1)

    inv = (1.0 / (10000.0 ** (np.arange(0, ROPE, 2, dtype=np.float32) / ROPE))).astype(np.float32)
    freq, sign = np.zeros((P, 1), np.float32), np.zeros((P, 1), np.float32)
    freq[64:96, 0] = np.concatenate([inv, inv])
    sign[64:96, 0] = np.repeat([-1.0, 1.0], 16)
    ffn_dw = np.concatenate([taps(interleave(a["ffn_dw"][l]).reshape(FTAPS, -1)) for l in range(2)], 1)
    parts = {
        "x_mixpre": columns(a["mix_pre_g"]), "mixpost": columns(a["mix_post_g"]), "ffnpre": columns(a["ffn_pre_g"]),
        "ffnpost": columns(a["ffn_post_g"]), "cm_b_in": columns(interleave(a["cm_b_in"][0])), "cm_dw": taps(a["cm_dw"][0]),
        "cm_dw_b": columns(a["cm_dw_b"]), "cm_ln_g": columns(a["cm_ln_g"]), "cm_ln_b": columns(a["cm_ln_b"]),
        "cm_b_out": columns(a["cm_b_out"]), "kv_g": columns(a["kv_norm_g"]), "ffn_dw": ffn_dw,
        "ffn_dw_b": columns(interleave(a["ffn_dw_b"])), "c": columns(a["c_2"]), "b_ada": columns(a["b_ada_2"]),
        "ffn1_g": columns(a["ffn1_norm_2"]), "mix_g": columns(a["mix_norm_2"]), "q_a": columns(a["q_a_norm_2"]),
        "kv_a": columns(a["kv_a_norm_2"]), "conv_w": np.concatenate([taps(a["conv_w_2"][l]) for l in range(2)], 1),
        "an_g": columns(a["attn_out_norm_2"]), "cn_g": columns(a["conv_out_norm_2"]), "ffn2_g": columns(a["ffn2_norm_2"]),
        "final_g": columns(a["final_norm_2"]), "inv_freq": freq, "rope_sign": sign}
    assert all(parts[n].shape == (P, c) for n, (_, c) in COLS.items()), {n: v.shape for n, v in parts.items()}
    m1, causal = masks()
    arrays = {
        "w": w,
        "ada": np.ascontiguousarray(a["w_ada_2"].reshape(2, KD, P, ADA_CHUNKS, ADA_CHUNK).transpose(0, 3, 1, 2, 4)
                                    ).reshape(-1, P, ADA_CHUNK),
        "cols": np.concatenate([parts[n] for n in COLS], 1),
        "x": np.ascontiguousarray(a["x"][0].T.reshape(KD, P, S).transpose(1, 0, 2)).reshape(P, KD * S),
        "pos": a["positions_2"].reshape(1, S), "ident": np.eye(P, dtype=np.float32), "masks1": m1, "causal": causal,
    }

    def program(known):
        nc = bacc.Bacc("TRN2", target_bir_lowering=False, num_devices=1)
        ins = {n: nc.dram_tensor(f"in_{n}", v.shape, mybir.dt.from_np(v.dtype), kind="ExternalInput").ap() for n, v in arrays.items()}
        out = nc.dram_tensor("result", (P, KD * S), F32, kind="ExternalOutput").ap()
        return nc, build(nc, ins, out, known)

    _, table = program(None)
    nc, _ = program(table)
    r = run_bass_kernel_spmd(nc, [{f"in_{n}": v for n, v in arrays.items()}], core_ids=[0])
    out = r.results[0]["result"].reshape(P, KD, S)
    return np.ascontiguousarray(out.transpose(2, 1, 0)).reshape(1, S, D)
```
